# Optimizing a Trainium2 kernel written in Bass

```python
import jax
import jax.numpy as jnp
from jax import lax
import numpy as np

D_MODEL = 1024
BATCH = 1
SEQ = 1024
DEPTH = 1

PLE_DIM = 256
GDN_HEADS = 4
GDN_HEAD_DIM = 128
GDN_WIDTH = GDN_HEADS * GDN_HEAD_DIM
GDN_CONV = 4
GDN_CHUNK = 64
SB_HEADS = 8
SB_HEAD_DIM = 64
SB_WIDTH = SB_HEADS * SB_HEAD_DIM
SB_BLOCK = 128
D_MIX = GDN_WIDTH + SB_WIDTH
IN_COLS = 4 * GDN_WIDTH + 2 * GDN_HEADS + 3 * SB_WIDTH
N_GROUPS = 8
EXPERTS_PER_GROUP = 8
N_EXPERTS = N_GROUPS * EXPERTS_PER_GROUP
TOP_K = 2
D_EXPERT = D_MODEL // 4
MOE_BLOCK = 128
EPS = 1e-6

kernel_name = 'hybrid_gdn_stickbreak_hmoe_block'

def rms_norm(x, w):
    xf = x.astype(jnp.float32)
    y = xf * lax.rsqrt(jnp.mean(xf * xf, axis=-1, keepdims=True) + EPS)
    return (y * w.astype(jnp.float32)).astype(x.dtype)

def l2_normalize(x):
    return x * lax.rsqrt(jnp.sum(x * x, axis=-1, keepdims=True) + EPS)

def causal_depthwise_conv_silu(u, w):
    k_width, channels = w.shape
    y = lax.conv_general_dilated(
        u, w[:, None, :].astype(u.dtype), window_strides=(1,),
        padding=[(k_width - 1, 0)], dimension_numbers=('NWC', 'WIO', 'NWC'),
        feature_group_count=channels)
    return jax.nn.silu(y)

def gated_deltanet(qkv, z, b, a, conv_w, a_log, dt_bias, norm_w):
    bsz, seq, _ = qkv.shape
    H, Dh, C = GDN_HEADS, GDN_HEAD_DIM, GDN_CHUNK
    n_chunks = seq // C
    qkv = causal_depthwise_conv_silu(qkv, conv_w).astype(jnp.float32)
    q, k, v = jnp.split(qkv, 3, axis=-1)
    q = l2_normalize(q.reshape(bsz, seq, H, Dh)) * (Dh ** -0.5)
    k = l2_normalize(k.reshape(bsz, seq, H, Dh))
    v = v.reshape(bsz, seq, H, Dh)
    beta = jax.nn.sigmoid(b.astype(jnp.float32))
    g = -jnp.exp(a_log.astype(jnp.float32)) * jax.nn.softplus(
        a.astype(jnp.float32) + dt_bias.astype(jnp.float32))

    def to_chunks(t):
        t = t.reshape((bsz, n_chunks, C, H) + t.shape[3:])
        return jnp.moveaxis(t, 3, 1)

    q, k, v, beta, g = (to_chunks(t) for t in (q, k, v, beta, g))
    gc = jnp.cumsum(g, axis=-1)
    incl = jnp.tril(jnp.ones((C, C), dtype=bool))
    strict = jnp.tril(jnp.ones((C, C), dtype=bool), k=-1)
    decay = jnp.exp(jnp.where(incl, gc[..., :, None] - gc[..., None, :], -jnp.inf))
    kk = jnp.einsum('bhnid,bhnjd->bhnij', k, k)
    lower = jnp.where(strict, beta[..., None] * kk * decay, 0.0)
    eye = jnp.eye(C, dtype=jnp.float32)
    rhs = jnp.concatenate([v * beta[..., None], k * (beta * jnp.exp(gc))[..., None]], axis=-1)
    sol = lax.linalg.triangular_solve(lower + eye, rhs, left_side=True, lower=True,
                                      unit_diagonal=True)
    u, w = sol[..., :Dh], sol[..., Dh:]
    qk = jnp.einsum('bhnid,bhnjd->bhnij', q, k) * decay
    xs = tuple(jnp.moveaxis(t, 2, 0) for t in (q, k, u, w, gc, qk))

    def chunk_step(state, inp):
        q_c, k_c, u_c, w_c, gc_c, qk_c = inp
        v_new = u_c - jnp.einsum('bhck,bhkv->bhcv', w_c, state)
        o_c = (jnp.einsum('bhck,bhkv->bhcv', q_c * jnp.exp(gc_c)[..., None], state)
               + jnp.einsum('bhcs,bhsv->bhcv', qk_c, v_new))
        g_last = gc_c[..., -1:]
        state = (state * jnp.exp(g_last)[..., None]
                 + jnp.einsum('bhck,bhcv->bhkv', k_c * jnp.exp(g_last - gc_c)[..., None], v_new))
        return state, o_c

    state0 = jnp.zeros((bsz, H, Dh, Dh), jnp.float32)
    _, o = lax.scan(chunk_step, state0, xs)
    o = jnp.transpose(o, (1, 0, 3, 2, 4)).reshape(bsz, seq, H, Dh)
    zf = z.astype(jnp.float32).reshape(bsz, seq, H, Dh)
    o = rms_norm(o, norm_w) * jax.nn.silu(zf)
    return o.reshape(bsz, seq, GDN_WIDTH)

def stick_breaking_attention(q, k, v):
    bsz, seq, _ = q.shape
    H, Dh = SB_HEADS, SB_HEAD_DIM

    def heads(t):
        return t.astype(jnp.float32).reshape(bsz, seq, H, Dh).transpose(0, 2, 1, 3)

    qh = heads(q) * (Dh ** -0.5)
    kh = heads(k)
    vh = heads(v)
    outs = []
    for blk in range(seq // SB_BLOCK):
        start, end = blk * SB_BLOCK, (blk + 1) * SB_BLOCK
        logits = jnp.einsum('bhtd,bhsd->bhts', qh[:, :, start:end], kh[:, :, :end])
        causal = jnp.arange(end)[None, :] < (start + jnp.arange(SB_BLOCK))[:, None]
        log_remain = jnp.where(causal, jax.nn.log_sigmoid(-logits), 0.0)
        log_after = lax.cumsum(log_remain, axis=3, reverse=True) - log_remain
        weights = jnp.where(causal, jnp.exp(jax.nn.log_sigmoid(logits) + log_after), 0.0)
        outs.append(jnp.einsum('bhts,bhsd->bhtd', weights, vh[:, :, :end]))
    o = jnp.concatenate(outs, axis=2)
    return o.transpose(0, 2, 1, 3)

def hierarchical_moe(h, w_rg, b_rg, w_re, b_re, w_gate, w_up, w_down):
    bsz, seq, d = h.shape
    n_tok = bsz * seq
    ht = h.reshape(n_tok, d)
    hf = ht.astype(jnp.float32)
    group_prob = jax.nn.softmax(hf @ w_rg.astype(jnp.float32) + b_rg.astype(jnp.float32), axis=-1)
    group_w, group_idx = lax.top_k(group_prob, 1)
    expert_logits = (hf @ w_re.astype(jnp.float32) + b_re.astype(jnp.float32)).reshape(
        n_tok, N_GROUPS, EXPERTS_PER_GROUP)
    in_group = jnp.take_along_axis(expert_logits, group_idx[:, :, None], axis=1)[:, 0]
    expert_prob = jax.nn.softmax(in_group, axis=-1)
    expert_w, expert_idx = lax.top_k(expert_prob, TOP_K)
    expert_w = expert_w / jnp.sum(expert_w, axis=-1, keepdims=True)
    gate = group_w * expert_w
    expert_id = group_idx * EXPERTS_PER_GROUP + expert_idx

    n_assign = n_tok * TOP_K
    eid = expert_id.reshape(n_assign)
    tok = jnp.repeat(jnp.arange(n_tok, dtype=jnp.int32), TOP_K)
    wts = gate.reshape(n_assign)
    order = jnp.argsort(eid)
    eid_s, tok_s, wts_s = eid[order], tok[order], wts[order]
    counts = jnp.bincount(eid, length=N_EXPERTS)
    starts = jnp.cumsum(counts) - counts
    padded = (counts + MOE_BLOCK - 1) // MOE_BLOCK * MOE_BLOCK
    padded_end = jnp.cumsum(padded)
    padded_start = padded_end - padded
    dest = padded_start[eid_s] + (jnp.arange(n_assign) - starts[eid_s])
    n_blocks = (n_assign + MOE_BLOCK - 1) // MOE_BLOCK + N_EXPERTS
    n_rows = n_blocks * MOE_BLOCK
    buf = jnp.zeros((n_rows, d), ht.dtype).at[dest].set(ht[tok_s])
    block_expert = jnp.minimum(
        jnp.searchsorted(padded_end, jnp.arange(n_blocks) * MOE_BLOCK, side='right'),
        N_EXPERTS - 1)

    def expert_block(args):
        xb, e = args
        hidden = jax.nn.silu(xb @ w_gate[e]) * (xb @ w_up[e])
        return hidden @ w_down[e]

    y_buf = lax.map(expert_block, (buf.reshape(n_blocks, MOE_BLOCK, d), block_expert))
    y_buf = y_buf.reshape(n_rows, d)
    out = jnp.zeros((n_tok, d), jnp.float32).at[tok_s].add(
        y_buf[dest].astype(jnp.float32) * wts_s[:, None])
    return out.reshape(bsz, seq, d).astype(h.dtype)

def setup_inputs(seed: int = 0) -> dict:
    key = jax.random.key(seed)
    ks = jax.random.split(key, 22)
    f32 = jnp.float32

    def normal(k, shape, scale):
        return jax.random.normal(k, shape, f32) * scale

    def gain(k, shape):
        return 1.0 + 0.02 * jax.random.normal(k, shape, f32)

    return {
        'x': normal(ks[0], (BATCH, SEQ, D_MODEL), 1.0),
        'p': normal(ks[1], (DEPTH, BATCH, SEQ, PLE_DIM), 1.0),
        'ln_mix': gain(ks[2], (DEPTH, D_MODEL)),
        'w_in': normal(ks[3], (DEPTH, D_MODEL, IN_COLS), D_MODEL ** -0.5),
        'conv_w': normal(ks[4], (DEPTH, GDN_CONV, 3 * GDN_WIDTH), GDN_CONV ** -0.5),
        'a_log': jnp.log(jax.random.uniform(ks[5], (DEPTH, GDN_HEADS), f32, 1.0, 16.0)),
        'dt_bias': normal(ks[6], (DEPTH, GDN_HEADS), 0.1),
        'gdn_norm_w': gain(ks[7], (DEPTH, GDN_HEAD_DIM)),
        'sb_norm_w': gain(ks[8], (DEPTH, SB_HEAD_DIM)),
        'w_out': normal(ks[9], (DEPTH, D_MIX, D_MODEL), D_MIX ** -0.5),
        'ln_moe': gain(ks[10], (DEPTH, D_MODEL)),
        'w_router_group': normal(ks[11], (DEPTH, D_MODEL, N_GROUPS), D_MODEL ** -0.5),
        'b_router_group': normal(ks[12], (DEPTH, N_GROUPS), 0.01),
        'w_router_expert': normal(ks[13], (DEPTH, D_MODEL, N_EXPERTS), D_MODEL ** -0.5),
        'b_router_expert': normal(ks[14], (DEPTH, N_EXPERTS), 0.01),
        'w_expert_gate': normal(ks[15], (DEPTH, N_EXPERTS, D_MODEL, D_EXPERT), D_MODEL ** -0.5),
        'w_expert_up': normal(ks[16], (DEPTH, N_EXPERTS, D_MODEL, D_EXPERT), D_MODEL ** -0.5),
        'w_expert_down': normal(ks[17], (DEPTH, N_EXPERTS, D_EXPERT, D_MODEL), D_EXPERT ** -0.5),
        'ln_ple': gain(ks[18], (DEPTH, D_MODEL)),
        'w_ple_gate': normal(ks[19], (DEPTH, D_MODEL, D_MODEL), D_MODEL ** -0.5),
        'w_ple_proj': normal(ks[20], (DEPTH, PLE_DIM, D_MODEL), PLE_DIM ** -0.5),
        'ln_final': gain(ks[21], (D_MODEL,)),
    }

def reference(x, p, ln_mix, w_in, conv_w, a_log, dt_bias, gdn_norm_w, sb_norm_w, w_out,
              ln_moe, w_router_group, b_router_group, w_router_expert, b_router_expert,
              w_expert_gate, w_expert_up, w_expert_down, ln_ple, w_ple_gate, w_ple_proj,
              ln_final):
    bsz, seq, _ = x.shape
    splits = np.cumsum([3 * GDN_WIDTH, GDN_WIDTH, GDN_HEADS, GDN_HEADS, SB_WIDTH, SB_WIDTH]).tolist()
    for i in range(DEPTH):
        h = rms_norm(x, ln_mix[i])
        proj = jnp.einsum('bsd,dc->bsc', h, w_in[i])
        gdn_qkv, gdn_z, gdn_b, gdn_a, sb_q, sb_k, sb_v = jnp.split(proj, splits, axis=-1)
        gdn_out = gated_deltanet(gdn_qkv, gdn_z, gdn_b, gdn_a, conv_w[i], a_log[i],
                                 dt_bias[i], gdn_norm_w[i])
        sb_out = rms_norm(stick_breaking_attention(sb_q, sb_k, sb_v), sb_norm_w[i])
        sb_out = sb_out.reshape(bsz, seq, SB_WIDTH)
        mixed = jnp.concatenate([gdn_out.astype(x.dtype), sb_out.astype(x.dtype)], axis=-1)
        x = x + jnp.einsum('bsc,cd->bsd', mixed, w_out[i])
        x = x + hierarchical_moe(rms_norm(x, ln_moe[i]), w_router_group[i], b_router_group[i],
                                 w_router_expert[i], b_router_expert[i], w_expert_gate[i],
                                 w_expert_up[i], w_expert_down[i])
        hp = rms_norm(x, ln_ple[i])
        ple_gate = jax.nn.sigmoid(jnp.einsum('bsd,de->bse', hp, w_ple_gate[i]).astype(jnp.float32))
        ple = jnp.einsum('bsp,pd->bsd', p[i], w_ple_proj[i]).astype(jnp.float32)
        x = x + (ple_gate * ple).astype(x.dtype)
    return rms_norm(x, ln_final)


_drawn_inputs = setup_inputs


def setup_inputs(seed=0):
    import zlib

    import numpy as np

    out = dict(_drawn_inputs(seed))
    spreads = {}
    factors = {'a_log': 5.089,
     'dt_bias': 8.0,
     'gdn_norm_w': 5.471,
     'sb_norm_w': 3.176,
     'ln_moe': 3.077,
     'b_router_group': 6.598,
     'b_router_expert': 6.183,
     'ln_ple': 8.0,
     'ln_final': 2.748}
    for name, (base, spread) in spreads.items():
        noise = np.random.default_rng([zlib.crc32(name.encode()), seed]).standard_normal(out[name].shape)
        drawn = base * np.exp(spread * noise) if base else spread * noise
        out[name] = jnp.asarray(drawn.astype(out[name].dtype))
    for name, factor in factors.items():
        out[name] = (out[name] * factor).astype(out[name].dtype)
    return out
```

```python
import numpy as np
import concourse.bass as bass
from concourse import mybir
from contextlib import ExitStack

F32 = mybir.dt.float32
BF16 = mybir.dt.bfloat16
I32 = mybir.dt.int32
U32 = mybir.dt.uint32
ALU = mybir.AluOpType
ACT = mybir.ActivationFunctionType
AX = mybir.AxisListType
ds = bass.ds

P = 128
SEQ, D = 1024, 1024
NT = SEQ // P
KT = D // P
GH, GD, CONV = 4, 128, 4
GW = GH * GD
SH, SD = 8, 64
SW = SH * SD
C_Z = 3 * GW
C_BA = C_Z + GW
C_SQ = C_BA + 2 * GH
C_SV = C_SQ + 2 * SW
IN_COLS = C_SV + SW
NQK = 2 * GH
NQKV = 3 * GH
NSQK = 2 * SW // P
TH = NT * GH
NG, EPG, NE, DE, PLE = 8, 8, 64, 256, 256
EPS = 1e-6
LEVELS = 7


def shape_constants():
    i = np.arange(P)
    row, col = i[:, None], i[None, :]
    consts = {
        "c_ident": np.eye(P, dtype=np.float32),
        "c_upto": (row <= col).astype(np.float32),
    }
    masks = np.zeros((P, LEVELS, 2, P), np.int32)
    for n in range(LEVELS):
        s = 1 << n
        m = ((row // s) == (col // s) + 1) & ((row // s) % 2 == 1)
        masks[:, n, 0] = m
        masks[:, n, 1] = m.T
    consts["c_masks"] = masks
    return consts


def stage_norm_and_project(nc, A, S):
    x, w_in = A["x"], A["w_in"][0]
    x_tok = x[0].rearrange("(t p) d -> p t d", p=P)
    w_v = w_in.rearrange("(p k) c -> p k c", k=KT)
    qkv_d, sqk_d = S["qkv_d"], S["sqk_d"]
    ident, v_sb, ba_sb, ssq_sb = S["ident"], S["v_sb"], S["ba_sb"], S["ssq_sb"]

    with ExitStack() as ctx:
        sb = lambda n, s, d=F32: ctx.enter_context(nc.sbuf_tensor(n, s, d))
        pb = lambda n, s, d=F32: ctx.enter_context(nc.psum_tensor(n, s, d))
        sems = []

        def sem(n):
            sems.append(nc.alloc_semaphore(n))
            return sems[-1]
        hT = sb("hT", [P, KT, SEQ])
        x_sb = sb("x_all", [P, NT, D])
        xn = sb("xn", [P, 2, D])
        sq_junk = sb("sq_junk", [P, D])
        ssx = sb("ssx", [P, NT])
        rsx = sb("rsx", [P, NT])
        lnw = sb("lnw", [P, KT])
        neghalf = sb("neghalf", [P, 1])
        taps_in = sb("taps_in", [CONV * NQKV, P])
        taps = sb("taps", [P, CONV, NQKV])
        ps_small = pb("ps_small", [P, 512])
        ps_taps = ps_small[:, 0:CONV * NQKV]
        pst = [pb(f"pst{i}", [P, KT, P]) for i in range(2)]

        x_in = [sem(f"x_in{i}") for i in range(NT)]
        small_in, taps_tr, ss_done, rs_pool, rs_done = sem("small_in"), sem("taps_tr"), sem("ss_done"), sem("rs_pool"), sem("rs_done")
        xn_done, xn_used, tr_done, hT_done, const_done = sem("xn_done"), sem("xn_used"), sem("tr_done"), sem("hT_done"), sem("const_done")

        with nc.Block() as block:
            @block.sync
            def _(sp):
                for t in range(NT):
                    sp.dma_start(x_sb[:, t, :], x_tok[:, t, :]).then_inc(x_in[t], 16)
                    if t == 0:
                        sp.dma_start(lnw[:], A["ln_mix"][0].rearrange("(p k) -> p k", k=KT)).then_inc(small_in, 16)
                        sp.dma_start(ident[:], A["c_ident"]).then_inc(small_in, 16)
                        sp.dma_start(taps_in[:], A["conv_w"][0].rearrange("j (c p) -> (j c) p", p=P)).then_inc(small_in, 16)

            @block.scalar
            def _(act):
                for t in range(NT):
                    act.wait_ge(x_in[t], 16)
                    if t >= 1:
                        act.wait_ge(ss_done, t)
                    act.activation(sq_junk[:], x_sb[:, t, :], ACT.Square,
                                   accum_out=ssx[:, t:t + 1]).then_inc(ss_done, 1)

            @block.gpsimd
            def _(pool):
                pool.memset(neghalf[:], -0.5).then_inc(const_done, 1)
                pool.wait_ge(const_done, 1)
                for t in range(NT):
                    pool.wait_ge(ss_done, t + 1)
                    pool.tensor_scalar(rsx[:, t:t + 1], ssx[:, t:t + 1], 1.0 / D, EPS, ALU.mult, ALU.add).then_inc(rs_pool, 1)
                    pool.wait_ge(rs_pool, t + 1)
                    pool.tensor_tensor(rsx[:, t:t + 1], rsx[:, t:t + 1], neghalf[:], ALU.pow).then_inc(rs_done, 1)

            @block.vector
            def _(dve):
                dve.wait_ge(small_in, 48)
                dve.wait_ge(taps_tr, 1)
                dve.tensor_copy(taps[:].rearrange("p j c -> p (j c)"), ps_taps)
                for t in range(NT + 1):
                    if t < NT:
                        dve.wait_ge(rs_done, t + 1)
                        if t >= 2:
                            dve.wait_ge(tr_done, t - 1)
                        dve.tensor_scalar(xn[:, t % 2, :], x_sb[:, t, :], rsx[:, t:t + 1], None, ALU.mult).then_inc(xn_done, 1)
                    if t >= 1:
                        u = t - 1
                        dve.wait_ge(tr_done, u + 1)
                        dve.tensor_tensor(hT[:, :, u * P:(u + 1) * P], pst[u % 2][:],
                                          lnw[:].unsqueeze(2).to_broadcast([P, KT, P]), ALU.mult).then_inc(hT_done, 1)

            @block.tensor
            def _(pe):
                pe.wait_ge(small_in, 48)
                pe.transpose(ps_taps, taps_in[:], ident[0:CONV * NQKV, 0:CONV * NQKV]).then_inc(taps_tr, 1)
                for t in range(NT):
                    pe.wait_ge(xn_done, t + 1)
                    if t >= 2:
                        pe.wait_ge(hT_done, t - 1)
                    for k in range(KT):
                        last = pe.transpose(pst[t % 2][:, k, :], xn[:, t % 2, k::KT], ident[:])
                    last.then_inc(tr_done, 1)

        w_ct = sb("w_ct", [P, 2, KT, P])
        w_tok = sb("w_tok", [P, 2, KT, GW])
        w_ba = sb("w_ba", [P, KT, 2 * GH])
        u_sb = sb("u_sb", [P, 2, CONV - 1 + SEQ])
        cacc = sb("cacc", [P, SEQ])
        y_sb = sb("y_sb", [P, 2, SEQ])
        z_sb = x_sb[:, 0:NT // 2, :].rearrange("p a (b n) -> p (a b) n", b=2)
        sq_sb = sb("sq_sb", [P, 2, SEQ])
        ones = sb("ones_p", [P, 1])
        ps = [pst[i][:].rearrange("p k n -> p (k n)") for i in range(2)]
        psn = ps_small[:, 64:64 + NT * NQK].rearrange("p (t c) -> p t c", t=NT)
        psb = ps_small[:, 128:128 + NT * 2 * GH].rearrange("p (t c) -> p t c", t=NT)
        psk = [pb("psk0", [P, GW]), pb("psk1", [P, GW])]
        NCT = NQKV + NSQK

        w_in_sem = [sem("w_in_even"), sem("w_in_odd")]
        y_stored = [sem("y_stored_even"), sem("y_stored_odd")]
        ch_done = sem("ch_done")
        ch_copied = sem("ch_copied")
        conv_done = sem("conv_done")
        conv_step = sem("conv_step")
        silu_done = sem("silu_done")
        sqr_done = sem("sqr_done")
        ssq_done = sem("ssq_done")
        wt_in, ba_in, ones_done, pad_done = sem("wt_in"), sem("ba_in"), sem("ones_done"), sem("pad_done")
        tok_done, tok_read, ba_done, ssq_read, z_stored = (sem(n) for n in ("tok_done", "tok_read", "ba_done", "ssq_read", "z_stored"))

        with nc.Block() as block:
            @block.sync
            def _(sp):
                def load_w(s, col):
                    sp.dma_start(w_ct[:, s], w_v[:, :, ds(col, P)]).then_inc(w_in_sem[s], 16)

                def store(s, dst, row):
                    sp.dma_start(dst[ds(row, P), :], y_sb[:, s]).then_inc(y_stored[s], 16)

                for s in range(2):
                    sp.sem_inc(y_stored[s], 16)
                    load_w(s, s * P)
                sp.dma_start(w_tok[:, 0], w_v[:, :, C_Z:C_Z + GW]).then_inc(wt_in, 16)
                sp.dma_start(w_tok[:, 1], w_v[:, :, C_SV:C_SV + SW]).then_inc(wt_in, 16)
                sp.dma_start(w_ba[:], w_v[:, :, C_BA:C_BA + 2 * GH]).then_inc(ba_in, 16)
                with sp.Fori(0, NQKV // 2 - 1) as j:
                    for s in range(2):
                        sp.wait_ge(ch_done, 2 * j + s + 1)
                        load_w(s, (2 * j + 2 + s) * P)
                        sp.wait_ge(silu_done, 2 * j + s + 2)
                        store(s, qkv_d, (2 * j + s) * P)
                for s in range(2):
                    ct = NQKV - 2 + s
                    sp.wait_ge(ch_done, ct + 1)
                    load_w(s, C_SQ + s * P)
                    sp.wait_ge(silu_done, ct + 2)
                    store(s, qkv_d, ct * P)
                with sp.Fori(0, NSQK // 2 - 1) as j:
                    for s in range(2):
                        sp.wait_ge(ch_done, 2 * j + NQKV + s + 1)
                        load_w(s, (2 * j + 2 + s) * P + C_SQ)
                        sp.wait_ge(ch_copied, 2 * j + NQKV + s + 3)
                        store(s, sqk_d, (2 * j + s) * P)
                for s in range(2):
                    sp.wait_ge(ch_copied, NCT - 2 + s + 3)
                    store(s, sqk_d, (NSQK - 2 + s) * P)
                sp.wait_ge(tok_read, NT)
                sp.dma_start(S["z_d"].rearrange("(t p) n -> p t n", p=P), z_sb).then_inc(z_stored, 16)
                for s in range(2):
                    sp.wait_ge(y_stored[s], 16 * (NCT // 2 + 1))
                sp.wait_ge(z_stored, 16)

            @block.tensor
            def _(pe):
                def project(ct, s, nth):
                    pe.wait_ge(w_in_sem[s], nth * 16 + 16)
                    pe.wait_ge(ch_copied, ct + 1)
                    for half in range(2):
                        cols = slice(half * 512, half * 512 + 512)
                        for k in range(KT):
                            last = pe.matmul(ps[s][:, cols], w_ct[:, s, k, :], hT[:, k, cols], start=k == 0, stop=k == KT - 1)
                    last.then_inc(ch_done, 1)

                def square_sums(ct, s):
                    pe.wait_ge(sqr_done, ct + 1)
                    for t in range(NT):
                        last = pe.matmul(psn[:, t, ds(ct, 1)], sq_sb[:, s, t * P:(t + 1) * P], ones[:], start=True, stop=True)
                    last.then_inc(ssq_done, 1)

                pe.wait_ge(ones_done, 1)
                pe.sem_inc(ssq_done, 2)
                project(0, 0, 0)
                with pe.Fori(0, NQK // 2) as j:
                    project(2 * j + 1, 1, j)
                    square_sums(2 * j, 0)
                    project(2 * j + 2, 0, j + 1)
                    square_sums(2 * j + 1, 1)
                with pe.Fori(0, (NCT - NQK) // 2 - 1) as j:
                    project(2 * j + NQK + 1, 1, j + NQK // 2)
                    project(2 * j + NQK + 2, 0, j + NQK // 2 + 1)
                project(NCT - 1, 1, NCT // 2 - 1)
                pe.wait_ge(wt_in, 32)
                for n in range(2):
                    for t in range(NT):
                        m = n * NT + t
                        if m >= 2:
                            pe.wait_ge(tok_read, m - 1)
                        for k in range(KT):
                            last = pe.matmul(psk[m % 2][:], hT[:, k, t * P:(t + 1) * P], w_tok[:, n, k, :],
                                             start=k == 0, stop=k == KT - 1)
                        last.then_inc(tok_done, 1)
                pe.wait_ge(ba_in, 16)
                pe.wait_ge(ssq_read, 1)
                for t in range(NT):
                    for k in range(KT):
                        last = pe.matmul(psb[:, t, :], hT[:, k, t * P:(t + 1) * P], w_ba[:, k, :],
                                         start=k == 0, stop=k == KT - 1)
                last.then_inc(ba_done, 1)

            @block.scalar
            def _(act):
                act.sem_inc(ch_copied, 2)
                act.sem_inc(silu_done, 1)
                act.wait_ge(pad_done, 2)

                def conv_and_silu(ct, s, nth):
                    act.wait_ge(ch_done, ct + 1)
                    act.wait_ge(conv_done, ct + 1)
                    act.activation(u_sb[:, s, CONV - 1:], ps[s], ACT.Copy).then_inc(ch_copied, 1)
                    act.wait_ge(conv_done, ct + 3)
                    act.wait_ge(y_stored[s], nth * 16 + 16)
                    act.activation(y_sb[:, s], cacc[:], ACT.Silu).then_inc(silu_done, 1)

                with act.Fori(0, NQK // 2) as j:
                    for s in range(2):
                        ct = 2 * j + s
                        conv_and_silu(ct, s, j)
                        act.wait_ge(silu_done, ct + 2)
                        act.wait_ge(ssq_done, ct + 1)
                        act.activation(sq_sb[:, s], y_sb[:, s], ACT.Square).then_inc(sqr_done, 1)
                with act.Fori(0, GH // 2) as j:
                    for s in range(2):
                        conv_and_silu(2 * j + NQK + s, s, j + NQK // 2)
                with act.Fori(0, NSQK // 2) as j:
                    for s in range(2):
                        act.wait_ge(ch_done, 2 * j + NQKV + s + 1)
                        act.wait_ge(y_stored[s], (j + NQKV // 2) * 16 + 16)
                        act.activation(y_sb[:, s], ps[s], ACT.Copy).then_inc(ch_copied, 1)
                for n in range(2):
                    for t in range(NT):
                        act.wait_ge(tok_done, n * NT + t + 1)
                        out, f = (z_sb, ACT.Silu) if n == 0 else (v_sb, ACT.Copy)
                        act.activation(out[:, t, :], psk[t % 2][:], f).then_inc(tok_read, 1)

            @block.vector
            def _(dve):
                dve.memset(ones[:], 1.0).then_inc(ones_done, 1)
                for s in range(2):
                    dve.memset(u_sb[:, s, 0:CONV - 1], 0.0).then_inc(pad_done, 1)
                dve.wait_ge(pad_done, 2)
                dve.sem_inc(conv_done, 2)
                with dve.Fori(0, NQKV // 2) as j:
                    for s in range(2):
                        ct = 2 * j + s
                        dve.wait_ge(ch_copied, ct + 3)
                        dve.wait_ge(silu_done, ct + 1)
                        dve.tensor_scalar(cacc[:], u_sb[:, s, CONV - 1:], taps[:, CONV - 1, ds(ct, 1)],
                                          None, ALU.mult).then_inc(conv_step, 1)
                        for i in range(CONV - 1):
                            dve.wait_ge(conv_step, ct * (CONV - 1) + (i + 1))
                            dve.scalar_tensor_tensor(cacc[:], u_sb[:, s, i:i + SEQ], taps[:, i, ds(ct, 1)], cacc[:],
                                                     ALU.mult, ALU.add).then_inc(conv_step if i < CONV - 2 else conv_done, 1)
                dve.wait_ge(ssq_done, NQK + 2)
                dve.tensor_copy(ssq_sb[:], psn).then_inc(ssq_read, 1)
                dve.wait_ge(ba_done, 1)
                dve.tensor_copy(ba_sb[:], psb)

        nc.clear_and_free_semaphores(sems)
        nc.all_engine_barrier()


def stage_gates(nc, A, S):
    ba_sb, ssq_sb, ident = S["ba_sb"], S["ssq_sb"], S["ident"]
    decay_qk, decay_kk, row_q, row_k = S["decay_qk"], S["decay_kk"], S["row_q"], S["row_k"]
    beta, col_kd, col_last = S["beta"], S["col_kd"], S["col_last"]
    with ExitStack() as ctx:
        sb = lambda n, s, d=F32: ctx.enter_context(nc.sbuf_tensor(n, s, d))
        pb = lambda n, s, d=F32: ctx.enter_context(nc.psum_tensor(n, s, d))
        sem = lambda n: ctx.enter_context(nc.semaphore(n))
        upto = sb("upto", [P, P])
        ones = sb("ones", [P, P])
        hp = sb("hp", [P, 2, GH])
        rate = sb("rate", [P, GH])
        arg = sb("arg", [P, NT, GH])
        mag = sb("mag", [P, NT, GH])
        y = sb("y_exp", [P, NT, GH])
        u = sb("u_exp", [P, NT, GH])
        um = sb("um_exp", [P, NT, GH])
        lu = sb("lu", [P, NT, GH])
        g = sb("g_dec", [P, TH])
        gc = sb("gc", [P, TH])
        dl = sb("dl", [P, TH])
        rt = sb("rt", [P, NT, NQK])
        r_q = sb("r_q", [P, TH])
        nb_k = sb("nb_k", [P, TH])
        r_k = sb("r_k", [P, TH])
        dec = sb("dec", [P, 2, GH, P])
        egr = sb("egr", [P, 2, GH, P])
        p_cum = pb("p_cum", [P, 2, TH])
        p_row = [pb(f"p_row{i}", [P, 3, 512]) for i in range(2)]
        const_in, hp_in = sem("gconst_in"), sem("hp_in")
        v_step, a_step, pe_cum, ones_ok = sem("v_step"), sem("a_step"), sem("pe_cum"), sem("ones_ok")
        rows_done, diff_done, exp_done, mat_done, sel_done = sem("rows_done"), sem("diff_done"), sem("exp_done"), sem("mat_done"), sem("sel_done")
        dk_done, egr_done = sem("dk_done"), sem("egr_done")
        VPRE = 17

        with nc.Block() as block:
            @block.sync
            def _(sp):
                sp.dma_start(hp[:, 0, :], A["a_log"][0:1, :].to_broadcast([P, GH])).then_inc(hp_in, 16)
                sp.dma_start(hp[:, 1, :], A["dt_bias"][0:1, :].to_broadcast([P, GH])).then_inc(hp_in, 16)
                sp.dma_start(upto[:], A["c_upto"]).then_inc(const_in, 16)

            @block.scalar
            def _(act):
                act.wait_ge(hp_in, 32)
                act.activation(rate[:], hp[:, 0, :], ACT.Exp).then_inc(a_step, 1)
                act.wait_ge(v_step, 2)
                act.activation(y[:], mag[:], ACT.Exp, scale=-1.0).then_inc(a_step, 1)
                act.wait_ge(v_step, 3)
                act.activation(lu[:], u[:], ACT.Ln).then_inc(a_step, 1)
                act.activation(beta[:], ba_sb[:, :, 0:GH], ACT.Sigmoid).then_inc(a_step, 1)
                act.wait_ge(v_step, 4)
                act.activation(rt[:], rt[:], ACT.Sqrt).then_inc(a_step, 1)
                act.wait_ge(v_step, VPRE - 1)
                act.activation(col_kd[:], dl[:], ACT.Exp).then_inc(a_step, 1)
                act.wait_ge(pe_cum, 1)
                act.activation(col_last[:], p_cum[:, 1, :], ACT.Exp).then_inc(a_step, 1)
                for c in range(NT):
                    act.wait_ge(rows_done, c + 1)
                    if c >= 2:
                        act.wait_ge(mat_done, c - 1)
                    act.activation(egr[:, c % 2].rearrange("p h i -> p (h i)"), p_row[c % 2][:, 0, :], ACT.Exp).then_inc(egr_done, 1)
                    act.wait_ge(diff_done, 2 * c + 2)
                    act.activation(dec[:, c % 2], dec[:, c % 2], ACT.Exp).then_inc(exp_done, 1)

            @block.vector
            def _(dve):
                step = [0]

                def link(op):
                    op.then_inc(v_step, 1)
                    step[0] += 1
                    dve.wait_ge(v_step, step[0])
                dve.memset(ones[:], 1.0).then_inc(ones_ok, 1)
                dve.wait_ge(hp_in, 32)
                link(dve.tensor_tensor(arg[:], ba_sb[:, :, GH:2 * GH], hp[:, 1, :].unsqueeze(1).to_broadcast([P, NT, GH]), ALU.add))
                link(dve.scalar_tensor_tensor(mag[:], arg[:], -1.0, arg[:], ALU.mult, ALU.max))
                dve.wait_ge(a_step, 2)
                link(dve.tensor_scalar(u[:], y[:], 1.0, None, ALU.add))
                link(dve.tensor_scalar(rt[:], ssq_sb[:], EPS, None, ALU.add))
                link(dve.tensor_scalar(um[:], u[:], -1.0, 1e-30, ALU.add, ALU.max))
                link(dve.reciprocal(um[:], um[:]))
                link(dve.tensor_tensor(um[:], um[:], y[:], ALU.mult))
                dve.wait_ge(a_step, 3)
                link(dve.tensor_tensor(lu[:], lu[:], um[:], ALU.mult))
                link(dve.scalar_tensor_tensor(um[:], u[:], 1.0, y[:], ALU.is_equal, ALU.mult))
                link(dve.tensor_tensor(lu[:], lu[:], um[:], ALU.max))
                link(dve.scalar_tensor_tensor(lu[:], arg[:], 0.0, lu[:], ALU.max, ALU.add))
                link(dve.scalar_tensor_tensor(g[:].rearrange("p (t h) -> p t h", h=GH), lu[:], -1.0,
                                              rate[:].unsqueeze(1).to_broadcast([P, NT, GH]), ALU.mult, ALU.mult))
                dve.wait_ge(a_step, 5)
                th = lambda x: x[:].rearrange("p (t h) -> p t h", h=GH)
                link(dve.reciprocal(rt[:], rt[:]))
                dve.tensor_scalar(th(r_q), rt[:, :, 0:GH], GD ** -0.5, None, ALU.mult)
                dve.tensor_copy(th(r_k), rt[:, :, GH:NQK])
                link(dve.scalar_tensor_tensor(th(nb_k), beta[:], -1.0, rt[:, :, GH:NQK], ALU.mult, ALU.mult))
                dve.wait_ge(pe_cum, 1)
                link(dve.tensor_copy(gc[:], p_cum[:, 0, :]))
                link(dve.tensor_tensor(dl[:], p_cum[:, 1, :], gc[:], ALU.subtract))
                assert step[0] == VPRE - 1
                dve.wait_ge(a_step, 6)
                link(dve.tensor_tensor(col_kd[:], col_kd[:], r_k[:], ALU.mult))

                def matrices(c):
                    b3 = lambda x: x[:, c * GH:(c + 1) * GH].unsqueeze(2).to_broadcast([P, GH, P])
                    row = lambda n: p_row[c % 2][:, n, :].rearrange("p (h i) -> p h i", h=GH)
                    hs = slice(c * GH, (c + 1) * GH)
                    dve.wait_ge(exp_done, c + 1)
                    dve.tensor_tensor(dec[:, c % 2], dec[:, c % 2], b3(r_k), ALU.mult).then_inc(dk_done, 1)
                    dve.tensor_tensor(row_q[:, hs], egr[:, c % 2], row(1), ALU.mult)
                    dve.tensor_tensor(row_k[:, hs], egr[:, c % 2], row(2), ALU.mult)
                    dve.wait_ge(dk_done, c + 1)
                    dve.tensor_tensor(decay_qk[:, hs], dec[:, c % 2], row(1), ALU.mult)
                    dve.tensor_tensor(decay_kk[:, hs], dec[:, c % 2], row(2), ALU.mult).then_inc(mat_done, 1)

                for c in range(NT + 1):
                    if c < NT:
                        row0 = p_row[c % 2][:, 0, :].rearrange("p (h i) -> p h i", h=GH)
                        dve.wait_ge(egr_done, c + 1)
                        if c >= 2:
                            dve.wait_ge(mat_done, c - 1)
                        dve.tensor_tensor(dec[:, c % 2], row0, gc[:, c * GH:(c + 1) * GH].unsqueeze(2).to_broadcast([P, GH, P]),
                                          ALU.subtract).then_inc(diff_done, 1)
                        dve.wait_ge(diff_done, 2 * c + 1)
                        dve.tensor_scalar(dec[:, c % 2], dec[:, c % 2], 0.0, None, ALU.min).then_inc(diff_done, 1)
                    if c >= 1:
                        matrices(c - 1)

            @block.gpsimd
            def _(pool):
                for c in range(NT):
                    hs = slice(c * GH, (c + 1) * GH)
                    pool.wait_ge(mat_done, c + 1)
                    pool.affine_select(out=decay_qk[:, hs], in_=decay_qk[:, hs], compare_op=ALU.is_ge, fill=0.0, base=0,
                                       pattern=[[0, GH], [1, P]], channel_multiplier=-1)
                    pool.affine_select(out=decay_kk[:, hs], in_=decay_kk[:, hs], compare_op=ALU.is_gt, fill=0.0, base=0,
                                       pattern=[[0, GH], [1, P]], channel_multiplier=-1)

            @block.tensor
            def _(pe):
                pe.wait_ge(const_in, 16)
                pe.wait_ge(ones_ok, 1)
                pe.wait_ge(v_step, 12)
                pe.matmul(p_cum[:, 0, :], upto[:], g[:], start=True, stop=True)
                pe.matmul(p_cum[:, 1, :], ones[:], g[:], start=True, stop=True).then_inc(pe_cum, 1)
                pe.wait_ge(v_step, 14)
                for c in range(NT):
                    if c >= 2:
                        pe.wait_ge(mat_done, c - 1)
                    for n, (col, rhs) in enumerate(((g, upto), (r_q, ident), (nb_k, ident))):
                        for h in range(GH):
                            i = c * GH + h
                            last = pe.matmul(p_row[c % 2][:, n, h * P:(h + 1) * P], col[:, i:i + 1].to_broadcast([P, P]), rhs[:],
                                             start=True, stop=True)
                    last.then_inc(rows_done, 1)


STRIPS = [(t, c0, min(c0 + 512, (t + 1) * P)) for t in range(NT) for c0 in ((512, 0) if t >= 4 else (0,))]
NS = len(STRIPS)


def stage_mixers(nc, A, S):
    ident, masks = S["ident"], S["masks"]
    decay_qk, decay_kk, row_q, row_k = S["decay_qk"], S["decay_kk"], S["row_q"], S["row_k"]
    beta, col_kd, col_last = S["beta"], S["col_kd"], S["col_last"]
    v_sb, mx = S["v_sb"], S["mx"]
    qkv_v = S["qkv_d"].rearrange("(n p) t -> p n t", p=P)
    sqk_v = S["sqk_d"].rearrange("(a h p) t -> p a h t", a=2, p=SD)
    assert SH == NT
    with ExitStack() as ctx:
        sb = lambda n, s, d=F32: ctx.enter_context(nc.sbuf_tensor(n, s, d))
        pb = lambda n, s, d=F32: ctx.enter_context(nc.psum_tensor(n, s, d))
        sem = lambda n: ctx.enter_context(nc.semaphore(n))
        gst = sb("gst", [P, 2, NQKV, P])
        LT, X, XT, Y = (sb(n, [P, GH, P]) for n in ("LT", "X", "XT", "Y"))
        QKT, vb, kd, qe, ke, R, VN = (sb(n, [P, GH, P]) for n in ("QKT", "vb", "kd", "qe", "ke", "Rr", "VN"))
        St, Sg = sb("St", [P, GH, P]), sb("Sg", [P, GH, P])
        GA, GB, GC = (pb(n, [P, GH, P]) for n in ("GA", "GB", "GC"))
        qk_st = sb("qk_st", [SD, 2, 2, SEQ])
        rem = sb("rem", [P, 2, 512])
        brk = sb("brk", [P, 2, 512])
        Pm = sb("Pm", [P, 2, SEQ + 1])
        wt = sb("wt", [P, 3, 512])
        wT = sb("wT", [P, 2, 512])
        negb = sb("negb", [P, P], BF16)
        identb = sb("identb", [P, P], BF16)
        LB = [pb(f"LB{i}", [P, 512]) for i in range(2)]
        TB = [pb(f"TB{i}", [P, 512]) for i in range(2)]
        OB = pb("OB", [P, NT, SD])

        chunk_in = [sem("chunk_in0"), sem("chunk_in1")]
        head_in = [sem("head_in0"), sem("head_in1")]
        setup = sem("m_setup")
        mask_in = sem("mask_in")
        passed = sem("passed")
        pool_step = sem("pool_step")
        kk_done, qk_done, vt_done, kt_done, lt_done = (sem(n) for n in ("kk_done", "qk_done", "vt_done", "kt_done", "lt_done"))
        y_done, z_done, ks_done, vn_done, o_done, ds_done = (sem(n) for n in ("y_done", "z_done", "ks_done", "vn_done", "o_done", "ds_done"))
        LT_ok, QKT_ok, vb_ok, kd_ok, X_ok, R_ok, Sg_ok, S_ok = (sem(n) for n in (
            "LT_ok", "QKT_ok", "vb_ok", "kd_ok", "X_ok", "R_ok", "Sg_ok", "S_ok"))
        Y_ok, VN_ok, O_ok, init_ok, qe_ok = (sem(n) for n in ("Y_ok", "VN_ok", "O_ok", "init_ok", "qe_ok"))
        log_done, sig_done, scan_done, w_done, tr_done, ev_done, pv_done, at_done = (sem(n) for n in (
            "log_done", "sig_done", "scan_done", "w_done", "wtr_done", "ev_done", "pv_done", "at_done"))
        STEPS = NS + 3
        LV = LEVELS - 1

        pieces = ["kk_qk", "vt_kt", "lt"] + [f"{a}{n}" for n in range(1, LEVELS) for a in "yz"] + ["ks", "vn", "ods"]

        def pieces_at(pos):
            return [p for n, p in enumerate(pieces) if n * (2 * STEPS) // len(pieces) == pos]

        def both(body, e):
            with e.Fori(0, NT // 2) as j:
                for s in range(2):
                    body(j, s, 2 * j + s)

        with nc.Block() as block:
            @block.sync
            def _(sp):
                def load(i, s):
                    sp.dma_start(gst[:, s], qkv_v[:, :, ds(i * P, P)]).then_inc(chunk_in[s], 16)
                    sp.dma_start(qk_st[:, s], sqk_v[:, :, ds(i, 1), :].rearrange("p a h t -> p a (h t)")).then_inc(head_in[s], 16)
                sp.dma_start(masks[:], A["c_masks"]).then_inc(mask_in, 16)
                load(0, 0)
                load(1, 1)
                with sp.Fori(0, NT // 2 - 1) as j:
                    for s in range(2):
                        i = 2 * j + s
                        sp.wait_ge(S_ok, i + 2)
                        sp.wait_ge(log_done, i * NS + NS)
                        sp.sem_inc(passed, 1)
                        sp.wait_ge(qe_ok, i + 1)
                        sp.sem_inc(passed, 1)
                        load(i + 2, s)

            @block.tensor
            def _(pe):
                hd = lambda x, h: x[:, h, :]

                def logits(i, s, j, k):
                    t, c0, c1 = STRIPS[k]
                    if k == 0:
                        pe.wait_ge(head_in[s], j * 16 + 16)
                    pe.wait_ge(sig_done, i * NS + (k + 1))
                    diag = c1 == (t + 1) * P
                    last = pe.matmul(LB[k % 2][:, 0:c1 - c0], qk_st[:, s, 0, t * P:(t + 1) * P], qk_st[:, s, 1, c0:c1],
                                     start=True, stop=not diag)
                    if diag:
                        last = pe.matmul(LB[k % 2][:, c1 - c0 - P:c1 - c0], identb[:], negb[:], start=False, stop=True)
                    last.then_inc(log_done, 1)

                def transposes(i, k):
                    t, c0, c1 = STRIPS[k]
                    pe.wait_ge(w_done, i * NS + (k + 3))
                    pe.wait_ge(ev_done, i * NS + (k + 1))
                    for b in range((c1 - c0) // P):
                        last = pe.transpose(TB[k % 2][:, b * P:(b + 1) * P], wt[:, k % 3, b * P:(b + 1) * P], ident[:])
                    last.then_inc(tr_done, 1)

                def weighted(i, k):
                    t, c0, c1 = STRIPS[k]
                    if k == 0:
                        pe.wait_ge(at_done, i + 1)
                    pe.wait_ge(ev_done, i * NS + (k + 3))
                    first = c1 == (t + 1) * P
                    n = (c1 - c0) // P
                    for b in range(n):
                        last = pe.matmul(OB[:, t, :], wT[:, k % 2, b * P:(b + 1) * P], v_sb[:, c0 // P + b, ds(i * SD, SD)],
                                         start=first and b == 0, stop=c0 == 0 and b == n - 1)
                    last.then_inc(pv_done, 1)

                def delta(piece, j, s, i):
                    q, k, v = gst[:, s, 0:GH], gst[:, s, GH:2 * GH], gst[:, s, 2 * GH:3 * GH]
                    if piece == "kk_qk":
                        pe.wait_ge(chunk_in[s], j * 16 + 16)
                        pe.wait_ge(S_ok, i + 1)
                        for h in range(GH):
                            last = pe.matmul(GA[:, h, :], hd(k, h), hd(k, h), start=True, stop=True)
                        last.then_inc(kk_done, 1)
                        pe.wait_ge(O_ok, i + 1)
                        for h in range(GH):
                            last = pe.matmul(GB[:, h, :], hd(k, h), hd(q, h), start=True, stop=True)
                        last.then_inc(qk_done, 1)
                    elif piece == "vt_kt":
                        for h in range(GH):
                            last = pe.transpose(GC[:, h, :], hd(v, h), ident[:])
                        last.then_inc(vt_done, 1)
                        pe.wait_ge(LT_ok, i + 1)
                        for h in range(GH):
                            last = pe.transpose(GA[:, h, :], hd(k, h), ident[:])
                        last.then_inc(kt_done, 1)
                    elif piece == "lt":
                        pe.wait_ge(QKT_ok, i + 1)
                        for h in range(GH):
                            last = pe.transpose(GB[:, h, :], LT[:, h, :], ident[:])
                        last.then_inc(lt_done, 1)
                        pe.wait_ge(vb_ok, i + 1)
                        pe.wait_ge(kd_ok, i + 1)
                    elif piece[0] == "y":
                        n = int(piece[1])
                        pe.wait_ge(X_ok, i * LEVELS + n)
                        for h in range(GH):
                            last = pe.matmul(GA[:, h, :], LT[:, h, :], X[:, h, :], start=True, stop=True)
                        last.then_inc(y_done, 1)
                    elif piece[0] == "z":
                        n = int(piece[1])
                        pe.wait_ge(Y_ok, i * LV + n)
                        if n < LV:
                            for h in range(GH):
                                pe.matmul(GB[:, h, :], XT[:, h, :], Y[:, h, :], start=True, stop=True)
                        for h in range(GH):
                            last = pe.matmul(GC[:, h, :], Y[:, h, :], XT[:, h, :], start=True, stop=True)
                        last.then_inc(z_done, 1)
                    elif piece == "ks":
                        pe.wait_ge(qe_ok, i + 1)
                        for h in range(GH):
                            last = pe.matmul(GA[:, h, :], ke[:, h, :], St[:, h, :], start=True, stop=True)
                        last.then_inc(ks_done, 1)
                    elif piece == "vn":
                        pe.wait_ge(R_ok, i + 1)
                        pe.wait_ge(X_ok, (i + 1) * LEVELS)
                        for h in range(GH):
                            last = pe.matmul(GC[:, h, :], XT[:, h, :], R[:, h, :], start=True, stop=True)
                        last.then_inc(vn_done, 1)
                    elif piece == "ods":
                        pe.wait_ge(VN_ok, i + 1)
                        for h in range(GH):
                            pe.matmul(GB[:, h, :], qe[:, h, :], St[:, h, :], start=True, stop=False)
                            last = pe.matmul(GB[:, h, :], QKT[:, h, :], VN[:, h, :], start=False, stop=True)
                        last.then_inc(o_done, 1)
                        for h in range(GH):
                            last = pe.matmul(GA[:, h, :], kd[:, h, :], VN[:, h, :], start=True, stop=True)
                        last.then_inc(ds_done, 1)

                pe.wait_ge(setup, 3)
                pe.wait_ge(pool_step, 4)
                pe.sem_inc(tr_done, 3)
                pe.sem_inc(pv_done, 2)
                pe.sem_inc(ds_done, 1)

                def body(j, s, i):
                    for k in range(STEPS):
                        if k < NS:
                            logits(i, s, j, k)
                        for p in pieces_at(2 * k):
                            delta(p, j, s, i)
                        if 2 <= k < NS + 2:
                            transposes(i, k - 2)
                        if 3 <= k:
                            weighted(i, k - 3)
                        for p in pieces_at(2 * k + 1):
                            delta(p, j, s, i)
                both(body, pe)

            @block.scalar
            def _(act):
                flat = lambda x: x[:].rearrange("p h n -> p (h n)")

                def breaks(i, k):
                    t, c0, c1 = STRIPS[k]
                    n = c1 - c0
                    act.wait_ge(log_done, i * NS + (k + 1))
                    act.wait_ge(w_done, i * NS + (k + 1))
                    act.activation(rem[:, k % 2, 0:n], LB[k % 2][:, 0:n], ACT.Sigmoid, scale=-SD ** -0.5)
                    act.activation(brk[:, k % 2, 0:n], LB[k % 2][:, 0:n], ACT.Sigmoid, scale=SD ** -0.5).then_inc(sig_done, 1)

                def evacuate(i, k):
                    t, c0, c1 = STRIPS[k]
                    n = c1 - c0
                    act.wait_ge(tr_done, i * NS + (k + 4))
                    act.wait_ge(pv_done, i * NS + (k + 1))
                    act.activation(wT[:, k % 2, 0:n], TB[k % 2][:, 0:n], ACT.Copy).then_inc(ev_done, 1)

                def delta(piece, i):
                    if piece[0] == "y":
                        n = int(piece[1])
                        act.wait_ge(y_done, i * LV + n)
                        if n == 1:
                            act.wait_ge(ds_done, i + 1)
                        act.activation(flat(Y), flat(GA), ACT.Copy).then_inc(Y_ok, 1)
                    elif piece == "vn":
                        act.wait_ge(vn_done, i + 1)
                        act.activation(flat(VN), flat(GC), ACT.Copy).then_inc(VN_ok, 1)
                    elif piece == "ods":
                        act.wait_ge(o_done, i + 1)
                        act.activation(mx[:, ds(i, 1), 0:GW].rearrange("p a n -> p (a n)"), flat(GB), ACT.Copy).then_inc(O_ok, 1)

                act.sem_inc(sig_done, 2)
                act.sem_inc(ev_done, 2)
                act.sem_inc(at_done, 1)
                act.sem_inc(O_ok, 1)

                def body(j, s, i):
                    for k in range(STEPS):
                        if k < NS:
                            breaks(i, k)
                        for p in pieces_at(2 * k):
                            delta(p, i)
                        if 2 <= k < NS + 2:
                            evacuate(i, k - 2)
                        for p in pieces_at(2 * k + 1):
                            delta(p, i)
                    act.wait_ge(pv_done, i * NS + (NS + 2))
                    act.activation(mx[:, :, ds(i * SD + GW, SD)], OB[:], ACT.Copy).then_inc(at_done, 1)
                both(body, act)

            @block.vector
            def _(dve):
                dve.memset(St[:], 0.0).then_inc(setup, 1)
                for n in range(2):
                    dve.memset(Pm[:, n, SEQ:SEQ + 1], 1.0).then_inc(setup, 1)
                dve.wait_ge(setup, 3)
                dve.sem_inc(S_ok, 1)
                dve.wait_ge(mask_in, 16)

                def scan(i, k):
                    t, c0, c1 = STRIPS[k]
                    n = c1 - c0
                    o = SEQ - (t + 1) * P
                    dve.wait_ge(sig_done, i * NS + (k + 3))
                    if t >= 4 and c0 == 0:
                        dve.wait_ge(scan_done, i * NS + k)
                    out = Pm[:, t % 2, o + c0:o + c1]
                    dve.tensor_tensor_scan(out[:, ::-1], rem[:, k % 2, 0:n][:, ::-1], rem[:, k % 2, 0:n][:, ::-1],
                                           Pm[:, t % 2, o + c1:o + c1 + 1], ALU.mult, ALU.bypass).then_inc(scan_done, 1)

                def delta(piece, j, s, i):
                    b3 = lambda x: x.rearrange("p t h -> p (t h)").unsqueeze(2).to_broadcast([P, GH, P])
                    hs = ds(i * GH, GH)
                    if piece == "kk_qk":
                        dve.wait_ge(kk_done, i + 1)
                        dve.tensor_tensor(LT[:], GA[:], decay_kk[:, hs, :], ALU.mult).then_inc(LT_ok, 1)
                        dve.wait_ge(qk_done, i + 1)
                        dve.tensor_tensor(QKT[:], GB[:], decay_qk[:, hs, :], ALU.mult).then_inc(QKT_ok, 1)
                    elif piece == "vt_kt":
                        dve.wait_ge(vt_done, i + 1)
                        dve.tensor_tensor(vb[:], GC[:], b3(beta[:, ds(i, 1), :]), ALU.mult).then_inc(vb_ok, 1)
                        dve.wait_ge(kt_done, i + 1)
                        dve.tensor_tensor(kd[:], GA[:], col_kd[:, hs].unsqueeze(2).to_broadcast([P, GH, P]), ALU.mult).then_inc(kd_ok, 1)
                    elif piece == "lt":
                        m = lambda n, tr: masks[:, n, tr, :].unsqueeze(1).to_broadcast([P, GH, P])
                        dve.wait_ge(init_ok, i + 1)
                        dve.wait_ge(lt_done, i + 1)
                        dve.sem_inc(passed, 1)
                        dve.copy_predicated(X[:], m(0, 0), GB[:])
                        dve.wait_ge(LT_ok, i + 1)
                        dve.sem_inc(passed, 1)
                        dve.copy_predicated(XT[:], m(0, 1), LT[:]).then_inc(X_ok, 1)
                    elif piece[0] == "z":
                        n = int(piece[1])
                        m = lambda tr: masks[:, n, tr, :].unsqueeze(1).to_broadcast([P, GH, P])
                        dve.wait_ge(z_done, i * LV + n)
                        dve.wait_ge(X_ok, i * LEVELS + n)
                        dve.sem_inc(passed, 1)
                        if n < LV:
                            dve.copy_predicated(X[:], m(0), GB[:])
                        dve.copy_predicated(XT[:], m(1), GC[:]).then_inc(X_ok, 1)
                    elif piece == "ks":
                        dve.wait_ge(S_ok, i + 1)
                        dve.tensor_tensor(Sg[:], St[:], col_last[:, hs].unsqueeze(2).to_broadcast([P, GH, P]), ALU.mult).then_inc(Sg_ok, 1)
                        dve.wait_ge(ks_done, i + 1)
                        dve.tensor_tensor(R[:], vb[:], GA[:], ALU.add).then_inc(R_ok, 1)
                    elif piece == "ods":
                        dve.wait_ge(ds_done, i + 2)
                        dve.wait_ge(Sg_ok, i + 1)
                        dve.tensor_tensor(St[:], Sg[:], GA[:], ALU.add).then_inc(S_ok, 1)

                def body(j, s, i):
                    for k in range(STEPS):
                        if k < NS:
                            if STRIPS[k][1] != 0 or STRIPS[k][0] < 4:
                                dve.wait_ge(w_done, i * NS + max(k - 1, 0) + 1)
                            scan(i, k)
                        for p in pieces_at(2 * k) + pieces_at(2 * k + 1):
                            delta(p, j, s, i)
                both(body, dve)

            @block.gpsimd
            def _(pool):
                pool.sem_inc(w_done, 2)
                pool.memset(negb[:], 0.0).then_inc(pool_step, 1)
                pool.memset(identb[:], 0.0).then_inc(pool_step, 1)
                pool.wait_ge(pool_step, 2)
                pool.affine_select(out=negb[:], in_=negb[:], compare_op=ALU.is_gt, fill=-1e30, base=0,
                                   pattern=[[-1, P]], channel_multiplier=1).then_inc(pool_step, 1)
                pool.affine_select(out=identb[:], in_=identb[:], compare_op=ALU.not_equal, fill=1.0, base=0,
                                   pattern=[[-1, P]], channel_multiplier=1).then_inc(pool_step, 1)
                pool.wait_ge(pool_step, 4)

                def weights(i, k):
                    t, c0, c1 = STRIPS[k]
                    n = c1 - c0
                    o = SEQ - (t + 1) * P
                    pool.wait_ge(scan_done, i * NS + (k + 1))
                    pool.wait_ge(tr_done, i * NS + (k + 1))
                    pool.tensor_tensor(wt[:, k % 3, 0:n], brk[:, k % 2, 0:n], Pm[:, t % 2, o + c0 + 1:o + c1 + 1],
                                       ALU.mult).then_inc(w_done, 1)

                def body(j, s, i):
                    for k in range(NS):
                        if k == 1:
                            pool.wait_ge(ds_done, i + 1)
                            ib = ident[:].unsqueeze(1).to_broadcast([P, GH, P])
                            pool.sem_inc(passed, 1)
                            pool.tensor_copy(X[:], ib)
                            pool.tensor_copy(XT[:], ib).then_inc(init_ok, 1)
                            pool.wait_ge(chunk_in[s], j * 16 + 16)
                            hs = ds(i * GH, GH)
                            pool.tensor_tensor(qe[:], gst[:, s, 0:GH], row_q[:, hs, :], ALU.mult)
                            pool.tensor_tensor(ke[:], gst[:, s, GH:2 * GH], row_k[:, hs, :], ALU.mult).then_inc(qe_ok, 1)
                        weights(i, k)
                both(body, pool)


CAP = 64
FAR = float(1 << 20)


def tiles_skewed(e, step):
    step(0, 0, 0, True, False)
    with e.Fori(0, NT // 2 - 1) as j:
        step(2 * j + 1, 1, j, False, False)
        step(2 * j + 2, 0, j + 1, False, False)
    step(NT - 1, 1, NT // 2 - 1, False, True)


def stage_output_projection(nc, A, S):
    ident, mx, lg_sb = (S[n] for n in ("ident", "mx", "lg_sb"))
    NR = NG + NE
    x_v = A["x"][0].rearrange("(t p) d -> p t d", p=P)
    z_v = S["z_d"].rearrange("(t p) n -> p t n", p=P)
    h_v = S["h_d"].rearrange("(t p) d -> p t d", p=P)
    with ExitStack() as ctx:
        sb = lambda n, s, d=F32: ctx.enter_context(nc.sbuf_tensor(n, s, d))
        pb = lambda n, s, d=F32: ctx.enter_context(nc.psum_tensor(n, s, d))
        sem = lambda n: ctx.enter_context(nc.semaphore(n))
        w_o = sb("w_o", [P, KT, D])
        x_sb = sb("o_x", [P, 2, D])
        z_sb = sb("o_z", [P, 2, GW])
        nw = sb("nw", [P, KT])
        w_r = sb("w_r", [P, KT, NR])
        b_r = sb("b_r", [P, NR])
        ln_row = sb("ln_row", [P, D])
        nh = sb("o_nh", [P, GH + SH])
        m_sb = sb("m_sb", [P, 2, D])
        msq = sb("msq", [P, D])
        mss = sb("mss", [P, 2, GH + SH])
        mT = sb("mT", [P, 2, KT, P])
        hss = sb("hss", [P, 2])
        hsq = sb("hsq", [P, D])
        h_sb = sb("h_sb", [P, 2, D])
        hT = sb("hT4", [P, KT, P])
        p_m = pb("p_m", [P, KT, P])
        p_h = pb("p_h", [P, KT, P])
        p_x = pb("p_x", [P, 2, 512])
        p_r = pb("p_r", [P, NR])
        wo_in, nw_in, small_in, wo_ok, const_ok = sem("wo_in"), sem("nw_in"), sem("r_in"), sem("wo_ok"), sem("o_const")
        msq_ok, ms_sum, ms_step, ms_ok, m_step, m_ok = (sem(n) for n in ("msq_ok", "ms_sum", "ms_step", "ms_ok", "m_step", "m_ok"))
        mtr_done, mT_ok, mm_done, x_ok, hs_ok, hp_step, hr_ok, h_ok = (sem(n) for n in (
            "mtr_done", "mT_ok", "mm_done", "x1_ok", "hs_ok", "hp_step", "hr_ok", "h_ok"))
        htr_done, hT_ok, r_done, lg_ok = (sem(n) for n in ("htr_done", "hT4_ok", "r_done", "lg_ok"))
        ple_in = sem("ple_in")
        x_in, z_in = [sem("o_x_in0"), sem("o_x_in1")], [sem("z_in0"), sem("z_in1")]
        passed = sem("o_passed")
        h_out = [sem("h_out0"), sem("h_out1")]

        with nc.Block() as block:
            @block.sync
            def _(sp):
                def load_rows(t, s):
                    sp.dma_start(x_sb[:, s], x_v[:, ds(t, 1), :].rearrange("p a d -> p (a d)")).then_inc(x_in[s], 16)
                    sp.dma_start(z_sb[:, s], z_v[:, ds(t, 1), :].rearrange("p a n -> p (a n)")).then_inc(z_in[s], 16)
                load_rows(0, 0)
                load_rows(1, 1)
                gv = A["gdn_norm_w"][0].rearrange("(q k) -> q k", k=KT)
                sv = A["sb_norm_w"][0].rearrange("(q k) -> q k", k=KT)
                ng, nq = GD // KT, SD // KT
                for r in range(GH):
                    sp.dma_start(nw[r * ng:(r + 1) * ng, :], gv).then_inc(nw_in, 16)
                for r in range(SH):
                    sp.dma_start(nw[P // 2 + r * nq:P // 2 + (r + 1) * nq, :], sv).then_inc(nw_in, 16)
                sp.dma_start(w_o[:], A["w_out"][0].rearrange("(p k) c -> p k c", k=KT)).then_inc(wo_in, 16)
                sp.dma_start(w_r[:, :, 0:NG], A["w_router_group"][0].rearrange("(p k) c -> p k c", k=KT)).then_inc(small_in, 16)
                sp.dma_start(w_r[:, :, NG:NR], A["w_router_expert"][0].rearrange("(p k) c -> p k c", k=KT)).then_inc(small_in, 16)
                sp.dma_start(b_r[:, 0:NG], A["b_router_group"][0:1, :].to_broadcast([P, NG])).then_inc(small_in, 16)
                sp.dma_start(b_r[:, NG:NR], A["b_router_expert"][0:1, :].to_broadcast([P, NE])).then_inc(small_in, 16)
                sp.dma_start(ln_row[:], A["ln_moe"][0:1, :].to_broadcast([P, D])).then_inc(small_in, 16)
                sp.dma_start(S["w_g"][:], A["w_ple_gate"][0].rearrange("(p k) c -> p k c", k=KT)).then_inc(ple_in, 16)
                sp.dma_start(S["lnp"][:], A["ln_ple"][0].rearrange("(p k) -> p k", k=KT)).then_inc(ple_in, 16)
                sp.sem_inc(h_out[0], 16)
                sp.sem_inc(h_out[1], 16)

                def store_h(t, s):
                    sp.wait_ge(h_ok, t + 1)
                    sp.dma_start(h_v[:, ds(t, 1), :].rearrange("p a d -> p (a d)"), h_sb[:, s]).then_inc(h_out[s], 16)
                with sp.Fori(0, NT // 2 - 1) as j:
                    for s in range(2):
                        sp.wait_ge(x_ok, 2 * j + s + 1)
                        load_rows(2 * j + s + 2, s)
                        store_h(2 * j + s, s)
                for s in range(2):
                    store_h(NT - 2 + s, s)
                for s in range(2):
                    sp.wait_ge(h_out[s], 16 * (NT // 2 + 1))
                sp.wait_ge(ple_in, 32)

            @block.gpsimd
            def _(pool):
                pool.memset(nh[:], -0.5).then_inc(const_ok, 1)
                pool.wait_ge(const_ok, 1)
                def heads_rms(t, s):
                    pool.wait_ge(ms_sum, t + 1)
                    pool.sem_inc(passed, 1)
                    pool.tensor_scalar(mss[:, s, 0:GH], mss[:, s, 0:GH], 1.0 / GD, EPS, ALU.mult, ALU.add)
                    pool.tensor_scalar(mss[:, s, GH:], mss[:, s, GH:], 1.0 / SD, EPS, ALU.mult, ALU.add).then_inc(ms_step, 1)
                    pool.wait_ge(ms_step, t + 1)
                    pool.tensor_tensor(mss[:, s], mss[:, s], nh[:], ALU.pow).then_inc(ms_ok, 1)

                def row_rms(t, s):
                    pool.wait_ge(hs_ok, t + 1)
                    pool.sem_inc(passed, 1)
                    pool.tensor_scalar(hss[:, s:s + 1], hss[:, s:s + 1], 1.0 / D, EPS, ALU.mult, ALU.add).then_inc(hp_step, 1)
                    pool.wait_ge(hp_step, t + 1)
                    pool.tensor_tensor(hss[:, s:s + 1], hss[:, s:s + 1], nh[:, 0:1], ALU.pow).then_inc(hr_ok, 1)

                def step(t, s, half_t, first, last):
                    if not last:
                        heads_rms(t + 1, 1 - s)
                    row_rms(t, s)
                heads_rms(0, 0)
                tiles_skewed(pool, step)

            @block.scalar
            def _(act):
                def mixed_squares(t, s, first):
                    if not first:
                        act.wait_ge(ms_sum, t)
                        act.sem_inc(passed, 1)
                    act.activation(msq[:, 0:GW], mx[:, ds(t, 1), 0:GW].rearrange("p a n -> p (a n)"), ACT.Square)
                    act.activation(msq[:, GW:], mx[:, ds(t, 1), GW:].rearrange("p a n -> p (a n)"), ACT.Square).then_inc(msq_ok, 1)

                def mixed_copy(t, s):
                    act.wait_ge(mtr_done, t + 1)
                    act.activation(mT[:, s].rearrange("p k n -> p (k n)"), p_m[:].rearrange("p k n -> p (k n)"), ACT.Copy).then_inc(mT_ok, 1)

                def h_squares(t, s):
                    act.wait_ge(x_ok, t + 1)
                    if not (isinstance(t, int) and t == 0):
                        act.wait_ge(hs_ok, t)
                    act.sem_inc(passed, 1)
                    act.activation(hsq[:], mx[:, ds(t, 1), :].rearrange("p a n -> p (a n)"), ACT.Square,
                                   accum_out=hss[:, s:s + 1]).then_inc(hs_ok, 1)

                def h_copy(t):
                    act.wait_ge(htr_done, t + 1)
                    act.activation(hT[:].rearrange("p k n -> p (k n)"), p_h[:].rearrange("p k n -> p (k n)"), ACT.Copy).then_inc(hT_ok, 1)

                def step(t, s, half_t, first, last):
                    if not last:
                        mixed_squares(t + 1, 1 - s, False)
                    if not first:
                        h_copy(t - 1)
                    if not last:
                        mixed_copy(t + 1, 1 - s)
                    h_squares(t, s)
                mixed_squares(0, 0, True)
                mixed_copy(0, 0)
                tiles_skewed(act, step)
                h_copy(NT - 1)

            @block.vector
            def _(dve):
                dve.wait_ge(nw_in, 16 * (GH + SH))
                dve.wait_ge(wo_in, 16)
                for k in range(KT):
                    last = dve.tensor_scalar(w_o[:, k, :], w_o[:, k, :], nw[:, k:k + 1], None, ALU.mult)
                last.then_inc(wo_ok, 1)

                def norm_mixed(t, s, n, nth):
                    dve.wait_ge(msq_ok, t + 1)
                    dve.tensor_reduce(mss[:, s, 0:GH], msq[:, 0:GW].rearrange("p (h n) -> p h n", h=GH), AX.X, ALU.add)
                    dve.tensor_reduce(mss[:, s, GH:], msq[:, GW:].rearrange("p (h n) -> p h n", h=SH), AX.X, ALU.add).then_inc(ms_sum, 1)
                    dve.wait_ge(ms_ok, t + 1)
                    if nth is not None:
                        dve.wait_ge(mtr_done, nth)
                    g, a = m_sb[:, s, 0:GW], m_sb[:, s, GW:]
                    dve.tensor_tensor(g.rearrange("p (h n) -> p h n", h=GH), mx[:, ds(t, 1), 0:GW].rearrange("p a (h n) -> p (a h) n", h=GH),
                                      mss[:, s, 0:GH].unsqueeze(2).to_broadcast([P, GH, GD]), ALU.mult).then_inc(m_step, 1)
                    dve.tensor_tensor(a.rearrange("p (h n) -> p h n", h=SH), mx[:, ds(t, 1), GW:].rearrange("p a (h n) -> p (a h) n", h=SH),
                                      mss[:, s, GH:].unsqueeze(2).to_broadcast([P, SH, SD]), ALU.mult)
                    dve.wait_ge(m_step, t + 1)
                    dve.wait_ge(z_in[s], n * 16 + 16)
                    dve.tensor_tensor(g, g, z_sb[:, s], ALU.mult).then_inc(m_ok, 1)

                def add_to_x(t, s, n):
                    xt = mx[:, ds(t, 1), :].rearrange("p a n -> p (a n)")
                    dve.wait_ge(mm_done, t + 1)
                    dve.wait_ge(x_in[s], n * 16 + 16)
                    dve.tensor_tensor(xt, x_sb[:, s], p_x[:].rearrange("p a n -> p (a n)"), ALU.add).then_inc(x_ok, 1)

                def norm_h(t, s, nth):
                    dve.wait_ge(hr_ok, t + 1)
                    dve.wait_ge(h_out[s], 16 * nth + 16)
                    if not (isinstance(t, int) and t < 2):
                        dve.wait_ge(htr_done, t - 1)
                    dve.scalar_tensor_tensor(h_sb[:, s], mx[:, ds(t, 1), :].rearrange("p a n -> p (a n)"), hss[:, s:s + 1],
                                             ln_row[:], ALU.mult, ALU.mult).then_inc(h_ok, 1)

                def biases(t):
                    dve.wait_ge(r_done, t + 1)
                    dve.tensor_tensor(lg_sb[:, ds(t, 1), :].rearrange("p a n -> p (a n)"), p_r[:], b_r[:], ALU.add).then_inc(lg_ok, 1)

                dve.wait_ge(small_in, 80)
                norm_mixed(0, 0, 0, None)
                norm_mixed(1, 1, 0, None)
                add_to_x(0, 0, 0)
                norm_h(0, 0, 0)
                with dve.Fori(0, NT // 2 - 1) as j:
                    norm_mixed(2 * j + 2, 0, j + 1, 2 * j + 1)
                    add_to_x(2 * j + 1, 1, j)
                    norm_h(2 * j + 1, 1, j)
                    biases(2 * j)
                    norm_mixed(2 * j + 3, 1, j + 1, 2 * j + 2)
                    add_to_x(2 * j + 2, 0, j + 1)
                    norm_h(2 * j + 2, 0, j + 1)
                    biases(2 * j + 1)
                add_to_x(NT - 1, 1, NT // 2 - 1)
                norm_h(NT - 1, 1, NT // 2 - 1)
                biases(NT - 2)
                biases(NT - 1)

            @block.tensor
            def _(pe):
                def mixed_transposes(t, s, first):
                    pe.wait_ge(m_ok, t + 1)
                    if not first:
                        pe.wait_ge(mT_ok, t)
                    for k in range(KT):
                        last = pe.transpose(p_m[:, k, :], m_sb[:, s, k::KT], ident[:])
                    last.then_inc(mtr_done, 1)

                def project(t, s, half):
                    for k in range(KT):
                        last = pe.matmul(p_x[:, half, :], mT[:, s, k, :], w_o[:, k, half * 512:half * 512 + 512],
                                         start=k == 0, stop=k == KT - 1)
                    if half:
                        last.then_inc(mm_done, 1)

                def h_transposes(t, s):
                    pe.wait_ge(h_ok, t + 1)
                    for k in range(KT):
                        last = pe.transpose(p_h[:, k, :], h_sb[:, s, k::KT], ident[:])
                    last.then_inc(htr_done, 1)

                def route(t):
                    pe.wait_ge(hT_ok, t + 1)
                    if not (isinstance(t, int) and t == 0):
                        pe.wait_ge(lg_ok, t)
                    for k in range(KT):
                        last = pe.matmul(p_r[:], hT[:, k, :], w_r[:, k, :], start=k == 0, stop=k == KT - 1)
                    last.then_inc(r_done, 1)

                def step(t, s, half_t, first, last):
                    pe.wait_ge(mT_ok, t + 1)
                    if not first:
                        pe.wait_ge(x_ok, t)
                    project(t, s, 0)
                    if not first:
                        h_transposes(t - 1, 1 - s)
                    if not last:
                        mixed_transposes(t + 1, 1 - s, False)
                    project(t, s, 1)
                    if not first:
                        route(t - 1)
                pe.wait_ge(wo_ok, 1)
                pe.wait_ge(small_in, 80)
                mixed_transposes(0, 0, True)
                tiles_skewed(pe, step)
                h_transposes(NT - 1, 1)
                route(NT - 1)


def stage_route(nc, A, S):
    lg, gates, onehot, rank, npass = (S[n] for n in ("lg_sb", "gates", "onehot", "rank", "npass"))
    with ExitStack() as ctx:
        sb = lambda n, s, d=F32: ctx.enter_context(nc.sbuf_tensor(n, s, d))
        pb = lambda n, s, d=F32: ctx.enter_context(nc.psum_tensor(n, s, d))
        sem = lambda n: ctx.enter_context(nc.semaphore(n))
        small = lambda n: sb(n, [P, NT, NG])
        one = lambda n: sb(n, [P, NT])
        i8 = sb("i8", [P, NG])
        gd, oh, cand, ing, tmp8 = small("r_gd"), small("r_oh"), small("r_cand"), small("r_ing"), small("r_tmp8")
        ge = small("r_ge")
        m, gi, gs, m2, e2, den, idx = one("r_m"), one("r_gi"), one("r_gs"), one("r_m2"), one("r_e2"), one("r_den"), sb("r_idx", [P, 2, NT])
        big = sb("r_big", [P, NT, EPG, NG])
        i64 = sb("i64", [P, NE])
        hot = sb("r_hot", [P, NT, NE], BF16)
        before = sb("before", [P, P], BF16)
        ones = sb("r_ones", [P, P], BF16)
        cmax = sb("cmax", [P, 1])
        ps_rank = pb("ps_rank", [P, NT, NE])
        ps_cnt = pb("ps_cnt", [P, NE])
        v, a, g_ok, pe_ok = sem("rt_v"), sem("rt_a"), sem("rt_pool"), sem("rt_pe")

        with nc.Block() as block:
            @block.gpsimd
            def _(pool):
                pool.iota(i8[:], pattern=[[1, NG]], base=-NG, channel_multiplier=0, allow_small_or_imprecise_dtypes=True).then_inc(g_ok, 1)
                pool.iota(i64[:], pattern=[[1, NE]], base=0, channel_multiplier=0, allow_small_or_imprecise_dtypes=True).then_inc(g_ok, 1)
                pool.memset(ones[:], 1.0).then_inc(g_ok, 1)
                pool.memset(before[:], 1.0).then_inc(g_ok, 1)
                pool.wait_ge(g_ok, 4)
                pool.affine_select(out=before[:], in_=before[:], compare_op=ALU.is_gt, fill=0.0, base=0,
                                   pattern=[[1, P]], channel_multiplier=-1).then_inc(g_ok, 1)

            @block.scalar
            def _(act):
                act.wait_ge(v, 2)
                act.activation(ge[:], gd[:], ACT.Exp).then_inc(a, 1)
                act.wait_ge(v, E2)
                act.activation(e2[:], m2[:], ACT.Exp).then_inc(a, 1)

            @block.vector
            def _(dve):
                n = [0]

                def link(op):
                    op.then_inc(v, 1)
                    n[0] += 1
                    dve.wait_ge(v, n[0])
                b = lambda x: x.unsqueeze(2).to_broadcast([P, NT, NG])
                i8b = i8[:].unsqueeze(1).to_broadcast([P, NT, NG])

                def first_of_max(x, out_idx):
                    link(dve.scalar_tensor_tensor(cand[:], x, 0.0, i8b, ALU.is_ge, ALU.mult))
                    link(dve.tensor_reduce(out_idx, cand[:], AX.X, ALU.min))
                    link(dve.tensor_tensor(oh[:], i8b, b(out_idx), ALU.is_equal))

                dve.wait_ge(g_ok, 5)
                link(dve.tensor_reduce(m[:], lg[:, :, 0:NG], AX.X, ALU.max))
                link(dve.tensor_tensor(gd[:], lg[:, :, 0:NG], b(m[:]), ALU.subtract))
                first_of_max(gd[:], gi[:])
                link(dve.tensor_tensor(big[:], lg[:, :, NG:].rearrange("p t (g e) -> p t e g", g=NG),
                                       oh[:].unsqueeze(2).to_broadcast([P, NT, EPG, NG]), ALU.mult))
                link(dve.tensor_reduce(ing[:], big[:], AX.X, ALU.add))
                link(dve.tensor_reduce(m[:], ing[:], AX.X, ALU.max))
                link(dve.tensor_tensor(ing[:], ing[:], b(m[:]), ALU.subtract))
                first_of_max(ing[:], idx[:, 0, :])
                link(dve.scalar_tensor_tensor(tmp8[:], oh[:], -3e38, ing[:], ALU.mult, ALU.add))
                link(dve.tensor_reduce(m2[:], tmp8[:], AX.X, ALU.max))
                assert n[0] == E2
                link(dve.tensor_tensor(tmp8[:], tmp8[:], b(m2[:]), ALU.subtract))
                first_of_max(tmp8[:], idx[:, 1, :])
                for k in range(2):
                    link(dve.scalar_tensor_tensor(idx[:, k, :], gi[:], float(EPG), idx[:, k, :], ALU.mult, ALU.add))
                    link(dve.tensor_scalar(idx[:, k, :], idx[:, k, :], float(NG * EPG + EPG), None, ALU.add))
                    link(dve.tensor_tensor(onehot[:, k], i64[:].unsqueeze(1).to_broadcast([P, NT, NE]),
                                           idx[:, k, :].unsqueeze(2).to_broadcast([P, NT, NE]), ALU.is_equal))
                link(dve.tensor_tensor(hot[:], onehot[:, 0], onehot[:, 1], ALU.add))
                assert n[0] == HOT
                dve.wait_ge(a, 2)
                link(dve.tensor_reduce(gs[:], ge[:], AX.X, ALU.add))
                link(dve.tensor_scalar(den[:], e2[:], 1.0, None, ALU.add))
                link(dve.tensor_tensor(den[:], den[:], gs[:], ALU.mult))
                link(dve.reciprocal(gates[:, 0, :], den[:]))
                link(dve.tensor_tensor(gates[:, 1, :], gates[:, 0, :], e2[:], ALU.mult))
                dve.wait_ge(pe_ok, 1)
                link(dve.tensor_reduce(cmax[:], ps_cnt[:], AX.X, ALU.max))
                link(dve.tensor_scalar(big[:, 0, 0:2, :].rearrange("p a b -> p (a b)"), i64[:, 0:SEQ // CAP], float(CAP), None, ALU.mult))
                link(dve.tensor_tensor(big[:, 1, 0:2, :].rearrange("p a b -> p (a b)"), big[:, 0, 0:2, :].rearrange("p a b -> p (a b)"),
                                       cmax[:].to_broadcast([P, SEQ // CAP]), ALU.is_lt))
                link(dve.tensor_reduce(cmax[:], big[:, 1, 0:2, :].rearrange("p a b -> p (a b)"), AX.X, ALU.add))
                link(dve.tensor_copy(npass[:], cmax[:]))
                for k in range(2):
                    link(dve.tensor_tensor(big[:].rearrange("p t a b -> p t (a b)"), onehot[:, k], ps_rank[:], ALU.mult))
                    link(dve.tensor_reduce(rank[:, k, :], big[:].rearrange("p t a b -> p t (a b)"), AX.X, ALU.add))

            @block.tensor
            def _(pe):
                pe.wait_ge(v, HOT)
                pe.wait_ge(g_ok, 5)
                for t in range(NT):
                    pe.matmul(ps_rank[:, t, :], before[:], hot[:, t, :], start=True, stop=t == 0)
                    for u in range(t):
                        pe.matmul(ps_rank[:, t, :], ones[:], hot[:, u, :], start=False, stop=u == t - 1)
                for t in range(NT):
                    last = pe.matmul(ps_cnt[:], ones[:], hot[:, t, :], start=t == 0, stop=t == NT - 1)
                last.then_inc(pe_ok, 1)


E2, HOT = 14, 25


def stage_experts(nc, A, S):
    onehot, rank, npass, ident = S["onehot"], S["rank"], S["npass"], S["ident"]
    h_d, y_d = S["h_d"], S["y_d"]
    R = 4
    wg = A["w_expert_gate"][0].rearrange("e (p k) f -> e p k f", k=KT)
    wu = A["w_expert_up"][0].rearrange("e (p k) f -> e p k f", k=KT)
    wdn = A["w_expert_down"][0].rearrange("e (p c) d -> e p c d", c=2)
    with ExitStack() as ctx:
        sb = lambda n, s, d=F32: ctx.enter_context(nc.sbuf_tensor(n, s, d))
        pb = lambda n, s, d=F32: ctx.enter_context(nc.psum_tensor(n, s, d))
        sem = lambda n: ctx.enter_context(nc.semaphore(n))
        w_g, lnp = S["w_g"], S["lnp"]
        w_gu = sb("w_gu", [P, R, 2, KT, DE])
        w_d = sb("w_d", [P, R, 2, D])
        slot_id = sb("slot_id", [P, P])
        choice = sb("choice", [P, 2, NT, 2])
        val = sb("val", [P, 2, 2, NT, NE])
        at_slot = sb("at_slot", [P, 2, NT, P])
        half_id = sb("half_id", [P, 1])
        empty = sb("empty", [P, 2, NE])
        tabf = sb("tabf", [P, 2, NE])
        tab = sb("tab", [P, 2, NE + 1], I32)
        token_at = sb("token_at", [CAP, 2], I32)
        row_at = sb("row_at", [P, 2], I32)
        pair = sb("pair", [P, CAP])
        xg = sb("xg", [CAP, 2, D])
        xT = sb("xT", [P, 2, KT, CAP])
        hs = sb("hs", [P, 2 * DE])
        sg = sb("sg", [P, 2, CAP])
        hT = sb("hTe", [P, 2, CAP])
        ys = sb("ys", [P, 2, 512])
        p_tab = pb("p_tab", [P, 2, NE])
        p_x = pb("pe_x", [P, KT, CAP])
        p_gu = pb("pe_gu", [P, 2 * DE])
        p_h = pb("pe_h", [P, 4, CAP])
        p_y = pb("pe_y", [P, 512])
        gu_in = [sem(f"gu_in{i}") for i in range(R)]
        dn_in = [sem(f"dn_in{i}") for i in range(R)]
        xg_in = [sem("xg_in0"), sem("xg_in1")]
        y_out = [sem("y_out0"), sem("y_out1")]
        pset, vset, token_ok, row_ok = sem("e_pset"), sem("e_vset"), sem("token_ok"), sem("row_ok")
        passed = sem("e_passed")
        hot_ok, tab_pe, tab_step, tab_ok = sem("hot_ok"), sem("tab_pe"), sem("tab_step"), sem("tab_ok")
        xt_done, xT_ok, gu_done, hs_ok, ht_done, sg_ok, hT_ok, y_done, ys_ok = (sem(n) for n in (
            "xt_done", "xT_ok", "gu_done", "ehs_ok", "ht_done", "sg_ok", "hTe_ok", "y_done", "ys_ok"))
        NX = NE + 1

        def passes(e, before_experts, body):
            n = e.value_load(npass[0:1, 0:1], min_val=1, max_val=SEQ // CAP)
            with e.Fori(0, n) as b:
                before_experts(b)
                with e.Fori(0, NE // R) as j:
                    for r in range(R):
                        body(b, j, r, j * R + r, b * NE + j * R + r)
            return n

        with nc.Block() as block:
            @block.sync
            def _(sp):
                def body(b, j, r, x, n):
                    sp.wait_ge(gu_done, n + 1)
                    sp.dma_start(w_gu[:, r, 0], wg[ds(x, 1)].rearrange("a p k f -> p (a k) f")).then_inc(gu_in[r], 16)
                    sp.dma_start(w_gu[:, r, 1], wu[ds(x, 1)].rearrange("a p k f -> p (a k) f")).then_inc(gu_in[r], 16)
                    sp.wait_ge(y_done, n + 1)
                    sp.dma_start(w_d[:, r], wdn[ds(x, 1)].rearrange("a p c d -> p (a c) d")).then_inc(dn_in[r], 16)
                passes(sp, lambda b: None, body)

            @block.gpsimd
            def _(pool):
                pool.iota(slot_id[:].rearrange("p (a n) -> p a n", a=2), pattern=[[0, 2], [1, CAP]], base=0, channel_multiplier=0,
                          allow_small_or_imprecise_dtypes=True).then_inc(pset, 1)
                for k in range(2):
                    pool.iota(choice[:, 0, :, k], pattern=[[2 * P, NT]], base=k + 1, channel_multiplier=2,
                              allow_small_or_imprecise_dtypes=True).then_inc(pset, 1)
                    pool.iota(choice[:, 1, :, k], pattern=[[P, NT]], base=1, channel_multiplier=1,
                              allow_small_or_imprecise_dtypes=True).then_inc(pset, 1)
                pool.memset(pair[:], 0.0).then_inc(pset, 1)
                pool.memset(half_id[:], 1.0).then_inc(pset, 1)
                pool.memset(tab[:, :, NE:], int(FAR)).then_inc(pset, 1)
                pool.memset(xg[:], 0.0).then_inc(pset, 1)
                pool.memset(row_at[:], int(FAR)).then_inc(pset, 1)
                pool.memset(ys[:], 0.0).then_inc(pset, 1)
                pool.wait_ge(pset, 11)
                pool.affine_select(out=pair[:], in_=pair[:], compare_op=ALU.not_equal, fill=1.0, base=0,
                                   pattern=[[-1, CAP]], channel_multiplier=1).then_inc(pset, 1)
                pool.affine_select(out=half_id[:], in_=half_id[:], compare_op=ALU.is_ge, fill=0.0, base=-CAP,
                                   pattern=[[0, 1]], channel_multiplier=1).then_inc(pset, 1)
                pool.wait_ge(pset, 13)
                pool.affine_select(out=pair[:], in_=pair[:], compare_op=ALU.not_equal, fill=1.0, base=-CAP,
                                   pattern=[[-1, CAP]], channel_multiplier=1).then_inc(pset, 1)
                for s in range(2):
                    pool.indirect_dma_start(out=y_d, out_offset=bass.IndirectOffsetOnAxis(ap=row_at[:, s:s + 1].bitcast(U32), axis=0),
                                            in_=ys[:, s, :], in_offset=None,
                                            bounds_check=4 * SEQ - 1, oob_is_err=False).then_inc(y_out[s], 16)

                def gather(b, x, s, n):
                    pool.wait_ge(xt_done, n + 1)
                    pool.sem_inc(passed, 1)
                    pool.tensor_copy(token_at[:, s:s + 1], tab[0:CAP, 1, ds(x, 1)]).then_inc(token_ok, 1)
                    pool.wait_ge(token_ok, n + 1)
                    pool.sem_inc(passed, 1)
                    pool.indirect_dma_start(out=xg[:, s, :], out_offset=None, in_=h_d,
                                            in_offset=bass.IndirectOffsetOnAxis(ap=token_at[:, s:s + 1].bitcast(U32), axis=0),
                                            bounds_check=SEQ - 1, oob_is_err=False).then_inc(xg_in[s], 16)

                def scatter(x, s, n, nth):
                    pool.wait_ge(y_out[s], nth * 16 + 16)
                    pool.sem_inc(passed, 1)
                    pool.tensor_copy(row_at[:, s:s + 1], tab[:, 0, ds(x, 1)]).then_inc(row_ok, 1)
                    pool.wait_ge(row_ok, n + 1)
                    pool.wait_ge(ys_ok, n + 2)
                    pool.sem_inc(passed, 1)
                    pool.indirect_dma_start(out=y_d, out_offset=bass.IndirectOffsetOnAxis(ap=row_at[:, s:s + 1].bitcast(U32), axis=0),
                                            in_=ys[:, s, :], in_offset=None,
                                            bounds_check=4 * SEQ - 1, oob_is_err=False).then_inc(y_out[s], 16)

                def before(b):
                    pool.wait_ge(tab_ok, b + 1)
                    gather(b, 0, 0, b * NX)

                def body(b, j, r, x, n):
                    gather(b, x + 1, (r + 1) % 2, b * NX + j * R + (r + 1))
                    scatter(x, r % 2, n, b * (NE // 2) + j * (R // 2) + r // 2)
                n = passes(pool, before, body)
                for s in range(2):
                    pool.wait_ge(y_out[s], n * (NE // 2 * 16) + 16)

            @block.tensor
            def _(pe):
                def tokens(b, s, n, nth):
                    pe.wait_ge(xg_in[s], nth * 16 + 16)
                    pe.wait_ge(xT_ok, n + 1)
                    pe.sem_inc(passed, 1)
                    for k in range(KT):
                        last = pe.transpose(p_x[:, k, :], xg[:, s, k::KT], ident[0:CAP, 0:CAP])
                    last.then_inc(xt_done, 1)

                def before(b):
                    pe.wait_ge(hot_ok, b + 1)
                    for i in range(2 * NT):
                        k, t = divmod(i, NT)
                        last = pe.matmul(p_tab[:].rearrange("p a e -> p (a e)"), at_slot[:, k, t, :],
                                         val[:, k, :, t, :], start=i == 0, stop=i == 2 * NT - 1)
                    last.then_inc(tab_pe, 1)
                    tokens(b, 0, b * NX, b * (NE // 2 + 1))

                def body(b, j, r, x, n):
                    q = b * NX + j * R + r
                    pe.wait_ge(gu_in[r], (b * (NE // R) + j) * 32 + 32)
                    pe.wait_ge(xT_ok, q + 2)
                    pe.wait_ge(hs_ok, n + 1)
                    for k in range(KT):
                        h = k % 2
                        last = pe.matmul(p_gu[h * CAP:(h + 1) * CAP, :], xT[:, r % 2, k, :], w_gu[:, r, :, k, :],
                                         start=k < 2, stop=k >= KT - 2)
                    last.then_inc(gu_done, 1)
                    s1 = (r + 1) % 2
                    nth = b * (NE // 2 + 1) + j * (R // 2) + (r + 1) // 2 if s1 == 0 else b * (NE // 2) + j * (R // 2) + r // 2
                    tokens(b, s1, q + 1, nth)
                    pe.wait_ge(hs_ok, n + 2)
                    pe.wait_ge(hT_ok, n + 1)
                    for a in range(2):
                        for c in range(2):
                            last = pe.matmul(p_h[:, 2 * a + c, :], hs[:, a * DE + c:(a + 1) * DE:2], pair[:], start=True, stop=True)
                    last.then_inc(ht_done, 1)
                    pe.wait_ge(dn_in[r], (b * (NE // R) + j) * 16 + 16)
                    pe.wait_ge(hT_ok, n + 2)
                    pe.wait_ge(ys_ok, n + 1)
                    for c in range(2):
                        for h in range(2):
                            last = pe.matmul(p_y[h * CAP:(h + 1) * CAP, :], hT[:, c, :], w_d[:, r, c, h * 512:(h + 1) * 512],
                                             start=c == 0, stop=c == 1)
                    last.then_inc(y_done, 1)
                pe.sem_inc(xt_done, 2)
                pe.sem_inc(ht_done, 1)
                pe.sem_inc(gu_done, R)
                pe.sem_inc(y_done, R)
                pe.wait_ge(pset, 14)
                passes(pe, before, body)

            @block.scalar
            def _(act):
                act.sem_inc(hs_ok, 1)
                for k in range(KT):
                    act.activation(w_g[:, k, :], w_g[:, k, :], ACT.Copy, scale=lnp[:, k:k + 1])

                def body(b, j, r, x, n):
                    act.wait_ge(gu_done, n + R + 1)
                    act.wait_ge(ht_done, n + 1)
                    act.activation(hs[:], p_gu[:], ACT.Copy).then_inc(hs_ok, 1)
                    act.wait_ge(ht_done, n + 2)
                    act.activation(sg[:], p_h[:, 0:2, :], ACT.Silu).then_inc(sg_ok, 1)
                passes(act, lambda b: None, body)

            @block.vector
            def _(dve):
                dve.sem_inc(xT_ok, 1)
                dve.sem_inc(hT_ok, 1)
                dve.sem_inc(ys_ok, 1)
                dve.wait_ge(pset, 14)
                for k in range(2):
                    for a in range(2):
                        dve.tensor_tensor(val[:, k, a], onehot[:, k], choice[:, a, :, k].unsqueeze(2).to_broadcast([P, NT, NE]),
                                          ALU.mult).then_inc(vset, 1)
                dve.wait_ge(vset, 4)

                def take(n, s):
                    dve.wait_ge(xt_done, n + 3)
                    dve.tensor_copy(xT[:, s], p_x[:]).then_inc(xT_ok, 1)

                def before(b):
                    for k in range(2):
                        last = dve.tensor_tensor(at_slot[:, k], slot_id[:].unsqueeze(1).to_broadcast([P, NT, P]),
                                                 rank[:, k, :].unsqueeze(2).to_broadcast([P, NT, P]), ALU.is_equal)
                    last.then_inc(hot_ok, 1)
                    dve.wait_ge(hot_ok, b + 1)
                    dve.tensor_scalar(rank[:], rank[:], -float(CAP), None, ALU.add).then_inc(tab_step, 1)
                    dve.wait_ge(tab_pe, b + 1)
                    dve.tensor_scalar(empty[:], p_tab[:], 0.0, FAR, ALU.is_equal, ALU.mult).then_inc(tab_step, 1)
                    dve.tensor_scalar(tabf[:, 0], p_tab[:, 0], -1.0, 2.0, ALU.add, ALU.mult).then_inc(tab_step, 1)
                    dve.wait_ge(tab_step, b * 6 + 3)
                    dve.tensor_scalar(tabf[:, 0], tabf[:, 0], half_id[:], None, ALU.add).then_inc(tab_step, 1)
                    dve.tensor_scalar(tabf[:, 1], p_tab[:, 1], -1.0, None, ALU.add).then_inc(tab_step, 1)
                    dve.wait_ge(tab_step, b * 6 + 5)
                    dve.tensor_tensor(tabf[:], tabf[:], empty[:], ALU.add).then_inc(tab_step, 1)
                    dve.wait_ge(tab_step, b * 6 + 6)
                    dve.wait_ge(y_out[0], b * (NE // 2) * 16 + 16)
                    dve.wait_ge(y_out[1], b * (NE // 2) * 16 + 16)
                    dve.tensor_copy(tab[:, :, 0:NE], tabf[:]).then_inc(tab_ok, 1)
                    take(b * NX, 0)

                def body(b, j, r, x, n):
                    take(b * NX + j * R + (r + 1), (r + 1) % 2)
                    dve.wait_ge(sg_ok, n + 1)
                    dve.wait_ge(y_done, n + R)
                    dve.tensor_tensor(hT[:], sg[:], p_h[:, 2:4, :], ALU.mult).then_inc(hT_ok, 1)
                    dve.wait_ge(y_done, n + R + 1)
                    dve.wait_ge(y_out[r % 2], (b * (NE // 2) + j * (R // 2) + r // 2) * 16 + 16)
                    dve.tensor_copy(ys[:, r % 2], p_y[:]).then_inc(ys_ok, 1)
                passes(dve, before, body)


def stage_per_layer_embedding(nc, A, S):
    ident, x_sb, gates, w_g = (S[n] for n in ("ident", "mx", "gates", "w_g"))
    y_v = S["y_d"].rearrange("(t p k h) n -> p t (k h n)", p=P, k=2, h=2)
    out_v = A["out"][0].rearrange("(t p) d -> p t d", p=P)
    p_v = A["p"][0, 0].rearrange("(t p) c -> p t c", p=P)
    PT = PLE // P
    with ExitStack() as ctx:
        sb = lambda n, s, d=F32: ctx.enter_context(nc.sbuf_tensor(n, s, d))
        pb = lambda n, s, d=F32: ctx.enter_context(nc.psum_tensor(n, s, d))
        sem = lambda n: ctx.enter_context(nc.semaphore(n))
        w_p = sb("w_p", [P, PT, D])
        lnf = sb("lnf", [P, D])
        nh = sb("f_nh", [P, 1])
        p_sb = sb("p_sb", [P, 2, PLE])
        pT = sb("pT", [P, 2, PT, P])
        y_sb = sb("y_sb7", [P, 2, 2, D])
        sq = sb("f_sq", [P, D])
        ss = sb("f_ss", [P, 2, 2])
        xn = sb("f_xn", [P, 2, D])
        xT = sb("f_xT", [P, 2, KT, P])
        gt = sb("f_gt", [P, D])
        o_sb = sb("o_sb", [P, 2, D])
        p_x = pb("f_px", [P, KT, P])
        p_g = pb("f_pg", [P, D])
        p_e = pb("f_pe", [P, D])
        p_p = pb("f_pp", [P, PT, P])
        passed = sem("f_passed")
        w_in, wp_in, nh_ok = sem("f_w_in"), sem("f_wp_in"), sem("f_nh_ok")
        p_in = [sem("f_p_in0"), sem("f_p_in1")]
        y_in, out_done = [sem("f_y_in0"), sem("f_y_in1")], [sem("out_done0"), sem("out_done1")]
        x2_step, x2_ok, s2_ok, r2_step, r2_ok, xn_ok, xt_done, xT_ok = (sem(n) for n in (
            "x2_step", "x2_ok", "s2_ok", "r2_step", "r2_ok", "f_xn_ok", "f_xt_done", "f_xT_ok"))
        pt_done, pT_ok, g_done, e_done, gt_ok, ge_ok, x3_ok, s3_ok, r3_step, r3_ok, o_ok = (sem(n) for n in (
            "pt_done", "pT_ok", "g_done", "e_done", "gt_ok", "ge_ok", "x3_ok", "s3_ok", "r3_step", "r3_ok", "o_ok"))
        xrow = lambda t: x_sb[:, ds(t, 1), :].rearrange("p a n -> p (a n)")

        with nc.Block() as block:
            @block.sync
            def _(sp):
                def load_y(t, s):
                    sp.dma_start(y_sb[:, s].rearrange("p k n -> p (k n)"), y_v[:, ds(t, 1), :].rearrange("p a n -> p (a n)")).then_inc(y_in[s], 16)
                    sp.dma_start(p_sb[:, s], p_v[:, ds(t, 1), :].rearrange("p a n -> p (a n)")).then_inc(p_in[s], 16)
                load_y(0, 0)
                sp.dma_start(w_p[:], A["w_ple_proj"][0].rearrange("(p k) c -> p k c", k=PT)).then_inc(wp_in, 16)
                sp.dma_start(lnf[:], A["ln_final"].unsqueeze(0).to_broadcast([P, D])).then_inc(w_in, 16)
                load_y(1, 1)
                sp.sem_inc(out_done[0], 16)
                sp.sem_inc(out_done[1], 16)

                def store(t, s):
                    sp.wait_ge(o_ok, t + 1)
                    sp.dma_start(out_v[:, ds(t, 1), :].rearrange("p a n -> p (a n)"), o_sb[:, s]).then_inc(out_done[s], 16)
                with sp.Fori(0, NT // 2 - 1) as j:
                    for s in range(2):
                        sp.wait_ge(x2_ok, 2 * j + s + 1)
                        sp.wait_ge(pt_done, 2 * j + s + 1)
                        load_y(2 * j + s + 2, s)
                        store(2 * j + s, s)
                for s in range(2):
                    store(NT - 2 + s, s)
                for s in range(2):
                    sp.wait_ge(out_done[s], 16 * (NT // 2 + 1))

            @block.gpsimd
            def _(pool):
                pool.memset(nh[:], -0.5).then_inc(nh_ok, 1)
                pool.wait_ge(nh_ok, 1)

                def rms(t, s, n, summed, mid, done):
                    c = ss[:, s, n:n + 1]
                    pool.wait_ge(summed, t + 1)
                    pool.sem_inc(passed, 1)
                    pool.tensor_scalar(c, c, 1.0 / D, EPS, ALU.mult, ALU.add).then_inc(mid, 1)
                    pool.wait_ge(mid, t + 1)
                    pool.tensor_tensor(c, c, nh[:], ALU.pow).then_inc(done, 1)
                rms(0, 0, 0, s2_ok, r2_step, r2_ok)
                with pool.Fori(0, NT // 2 - 1) as j:
                    for s in range(2):
                        rms(2 * j + s + 1, 1 - s, 0, s2_ok, r2_step, r2_ok)
                        rms(2 * j + s, s, 1, s3_ok, r3_step, r3_ok)
                rms(NT - 1, 1, 0, s2_ok, r2_step, r2_ok)
                rms(NT - 2, 0, 1, s3_ok, r3_step, r3_ok)
                rms(NT - 1, 1, 1, s3_ok, r3_step, r3_ok)

            @block.scalar
            def _(act):
                def before(t, s, first):
                    act.wait_ge(x2_ok, t + 1)
                    if not first:
                        act.wait_ge(s2_ok, t)
                    act.sem_inc(passed, 1)
                    act.activation(sq[:], xrow(t), ACT.Square, accum_out=ss[:, s, 0:1]).then_inc(s2_ok, 1)
                    act.wait_ge(pt_done, t + 1)
                    act.activation(pT[:, s].rearrange("p k n -> p (k n)"), p_p[:].rearrange("p k n -> p (k n)"), ACT.Copy).then_inc(pT_ok, 1)
                    act.wait_ge(xt_done, t + 1)
                    act.activation(xT[:, s].rearrange("p k n -> p (k n)"), p_x[:].rearrange("p k n -> p (k n)"), ACT.Copy).then_inc(xT_ok, 1)

                def after(t, s, first):
                    act.wait_ge(g_done, t + 1)
                    if not first:
                        act.wait_ge(x3_ok, t)
                    act.activation(gt[:], p_g[:], ACT.Sigmoid).then_inc(gt_ok, 1)
                    act.wait_ge(x3_ok, t + 1)
                    act.wait_ge(s2_ok, NT if isinstance(t, int) and t == NT - 1 else t + 2)
                    act.sem_inc(passed, 1)
                    act.activation(sq[:], xrow(t), ACT.Square, accum_out=ss[:, s, 1:2]).then_inc(s3_ok, 1)

                def step(t, s, half_t, first, last):
                    if not last:
                        before_next(t, s)
                    after(t, s, first)

                def before_next(t, s):
                    if not (isinstance(t, int) and t == 0):
                        act.wait_ge(s3_ok, t)
                    before(t + 1, 1 - s, False)
                before(0, 0, True)
                tiles_skewed(act, step)

            @block.vector
            def _(dve):
                def combine(t, s, nth):
                    dve.wait_ge(y_in[s], nth * 16 + 16)
                    dve.scalar_tensor_tensor(xrow(t), y_sb[:, s, 0], gates[:, 0, ds(t, 1)], xrow(t), ALU.mult, ALU.add).then_inc(x2_step, 1)
                    dve.wait_ge(x2_step, t + 1)
                    dve.scalar_tensor_tensor(xrow(t), y_sb[:, s, 1], gates[:, 1, ds(t, 1)], xrow(t), ALU.mult, ALU.add).then_inc(x2_ok, 1)
                    dve.wait_ge(r2_ok, t + 1)
                    if not (isinstance(t, int) and t < 2):
                        dve.wait_ge(xt_done, t - 1)
                    dve.tensor_scalar(xn[:, s], xrow(t), ss[:, s, 0:1], None, ALU.mult).then_inc(xn_ok, 1)

                def embed(t, s):
                    dve.wait_ge(gt_ok, t + 1)
                    dve.wait_ge(e_done, t + 1)
                    dve.tensor_tensor(gt[:], gt[:], p_e[:], ALU.mult).then_inc(ge_ok, 1)
                    dve.wait_ge(ge_ok, t + 1)
                    dve.tensor_tensor(xrow(t), xrow(t), gt[:], ALU.add).then_inc(x3_ok, 1)

                def finish(t, s, nth):
                    dve.wait_ge(r3_ok, t + 1)
                    dve.wait_ge(out_done[s], nth * 16 + 16)
                    dve.scalar_tensor_tensor(o_sb[:, s], xrow(t), ss[:, s, 1:2], lnf[:], ALU.mult, ALU.mult).then_inc(o_ok, 1)

                dve.wait_ge(w_in, 16)
                combine(0, 0, 0)
                combine(1, 1, 0)
                embed(0, 0)
                with dve.Fori(0, NT // 2 - 1) as j:
                    combine(2 * j + 2, 0, j + 1)
                    finish(2 * j, 0, j)
                    embed(2 * j + 1, 1)
                    combine(2 * j + 3, 1, j + 1)
                    finish(2 * j + 1, 1, j)
                    embed(2 * j + 2, 0)
                finish(NT - 2, 0, NT // 2 - 1)
                embed(NT - 1, 1)
                finish(NT - 1, 1, NT // 2 - 1)

            @block.tensor
            def _(pe):
                def transposes(t, s, first, nth):
                    pe.wait_ge(p_in[s], nth * 16 + 16)
                    if not first:
                        pe.wait_ge(pT_ok, t)
                    for k in range(PT):
                        last = pe.transpose(p_p[:, k, :], p_sb[:, s, k::PT], ident[:])
                    last.then_inc(pt_done, 1)
                    pe.wait_ge(xn_ok, t + 1)
                    if not first:
                        pe.wait_ge(xT_ok, t)
                    for k in range(KT):
                        last = pe.transpose(p_x[:, k, :], xn[:, s, k::KT], ident[:])
                    last.then_inc(xt_done, 1)

                def gate(t, s, half):
                    c = slice(half * 512, half * 512 + 512)
                    for k in range(KT):
                        last = pe.matmul(p_g[:, c], xT[:, s, k, :], w_g[:, k, c], start=k == 0, stop=k == KT - 1)
                    if half:
                        last.then_inc(g_done, 1)

                def project(t, s):
                    for half in range(2):
                        c = slice(half * 512, half * 512 + 512)
                        for k in range(PT):
                            last = pe.matmul(p_e[:, c], pT[:, s, k, :], w_p[:, k, c], start=k == 0, stop=k == PT - 1)
                    last.then_inc(e_done, 1)

                def step(t, s, half_t, first, last):
                    pe.wait_ge(xT_ok, t + 1)
                    pe.wait_ge(pT_ok, t + 1)
                    if not first:
                        pe.wait_ge(gt_ok, t)
                    gate(t, s, 0)
                    if not last:
                        transposes(t + 1, 1 - s, False, half_t + s)
                    gate(t, s, 1)
                    if not first:
                        pe.wait_ge(ge_ok, t)
                    project(t, s)
                pe.wait_ge(wp_in, 16)
                transposes(0, 0, True, 0)
                tiles_skewed(pe, step)


def build_program(nc, A):
    dram = lambda n, s: nc.dram_tensor(n, s, F32, kind="Internal").ap()
    S = {"qkv_d": dram("qkv_d", [3 * GW, SEQ]), "sqk_d": dram("sqk_d", [2 * SW, SEQ]), "z_d": dram("z_d", [SEQ, GW]),
         "h_d": dram("h_d", [SEQ, D]), "y_d": dram("y_d", [4 * SEQ, D // 2])}
    with ExitStack() as whole:
        def keep(stack, name, shape, dtype=F32):
            S[name] = stack.enter_context(nc.sbuf_tensor(name, shape, dtype))
        keep(whole, "ident", [P, P])
        keep(whole, "mx", [P, NT, D])
        with ExitStack() as mixing:
            keep(mixing, "v_sb", [P, NT, SW])
            keep(mixing, "ba_sb", [P, NT, 2 * GH])
            keep(mixing, "ssq_sb", [P, NT, NQK])
            stage_norm_and_project(nc, A, S)
            for name in ("decay_qk", "decay_kk", "row_q", "row_k"):
                keep(mixing, name, [P, TH, P])
            keep(mixing, "beta", [P, NT, GH])
            keep(mixing, "col_kd", [P, TH])
            keep(mixing, "col_last", [P, TH])
            keep(mixing, "masks", [P, LEVELS, 2, P], I32)
            stage_gates(nc, A, S)
            stage_mixers(nc, A, S)
        keep(whole, "gates", [P, 2, NT])
        keep(whole, "w_g", [P, KT, D])
        keep(whole, "lnp", [P, KT])
        with ExitStack() as moe:
            keep(moe, "onehot", [P, 2, NT, NE])
            keep(moe, "rank", [P, 2, NT])
            keep(moe, "npass", [P, 1], I32)
            keep(moe, "lg_sb", [P, NT, NG + NE])
            stage_output_projection(nc, A, S)
            stage_route(nc, A, S)
            stage_experts(nc, A, S)
        stage_per_layer_embedding(nc, A, S)


def kernel(**inputs):
    import concourse.bacc as bacc
    from concourse.bass_utils import run_bass_kernel_spmd

    nc = bacc.Bacc("TRN2", target_bir_lowering=False, num_devices=1)
    arrays, A = {}, {}
    for name, a in {**inputs, **shape_constants()}.items():
        a = np.ascontiguousarray(a)
        arrays[f"in_{name}"] = a
        A[name] = nc.dram_tensor(f"in_{name}", a.shape, mybir.dt.from_np(a.dtype), kind="ExternalInput").ap()
    A["out"] = nc.dram_tensor("out_0", (1, SEQ, D), F32, kind="ExternalOutput").ap()
    build_program(nc, A)
    r = run_bass_kernel_spmd(nc, [arrays], core_ids=[0])
    return r.results[0]["out_0"]
```
